# Optimizing a Trainium2 kernel written in Bass

```python
import jax, jax.numpy as jnp
from jax import lax
import numpy as np

D_MODEL = 1024
BATCH = 1
SEQ = 256
DEPTH = 1

D_CONV = D_MODEL
CONV_W = 3
N_HEADS = 8
HEAD_DIM = 128
D_ATTN = N_HEADS * HEAD_DIM
MOBA_BLOCK = 256
MOBA_TOPK = 3
Q_CHUNK = 64
D_FF = 2816
EPS = 1e-6
D_IN = 3 * D_CONV + 3 * D_ATTN + 2 * D_MODEL

kernel_name = "hybrid_conv_moba_gated_block"

def rmsnorm(x, g):
    x32 = x.astype(jnp.float32)
    y = x32 * lax.rsqrt(jnp.mean(x32 * x32, axis=-1, keepdims=True) + EPS)
    return y.astype(x.dtype) * g

def causal_dwconv(x, w):
    s = x.shape[1]
    xp = jnp.pad(x, ((0, 0), (CONV_W - 1, 0), (0, 0)))
    y = w[0] * xp[:, 0:s]
    for j in range(1, CONV_W):
        y = y + w[j] * xp[:, j:j + s]
    return y

def moba_attention(q, k, v):
    b, h, s, hd = q.shape
    nb = -(-s // MOBA_BLOCK)
    s_pad = nb * MOBA_BLOCK
    pad = ((0, 0), (0, 0), (0, s_pad - s), (0, 0))
    kp = jnp.pad(k, pad)
    vp = jnp.pad(v, pad)
    kb = kp.reshape(b, h, nb, MOBA_BLOCK, hd)
    vb = vp.reshape(b, h, nb, MOBA_BLOCK, hd)
    kbar = jnp.mean(kb.astype(jnp.float32), axis=3).astype(k.dtype)
    n_sel = min(MOBA_TOPK, nb)
    scale = hd ** -0.5
    bidx = jnp.arange(b)[:, None, None, None]
    hidx = jnp.arange(h)[None, :, None, None]

    def one_chunk(c):
        q0 = c * Q_CHUNK
        qc = lax.dynamic_slice_in_dim(q, q0, Q_CHUNK, axis=2)
        qpos = q0 + jnp.arange(Q_CHUNK)
        cur = q0 // MOBA_BLOCK
        gate = jnp.einsum('bhqd,bhnd->bhqn', qc, kbar).astype(jnp.float32)
        gate = jnp.where(jnp.arange(nb) < cur, gate, -jnp.inf)
        _, idx = lax.top_k(gate, n_sel)
        valid = jnp.arange(n_sel) < cur
        kg = kb[bidx, hidx, idx]
        vg = vb[bidx, hidx, idx]
        s_sel = jnp.einsum('bhqd,bhqnld->bhqnl', qc, kg).astype(jnp.float32) * scale
        s_sel = jnp.where(valid[:, None], s_sel, -jnp.inf).reshape(b, h, Q_CHUNK, n_sel * MOBA_BLOCK)
        k_own = lax.dynamic_slice_in_dim(kp, cur * MOBA_BLOCK, MOBA_BLOCK, axis=2)
        v_own = lax.dynamic_slice_in_dim(vp, cur * MOBA_BLOCK, MOBA_BLOCK, axis=2)
        kpos = cur * MOBA_BLOCK + jnp.arange(MOBA_BLOCK)
        s_own = jnp.einsum('bhqd,bhkd->bhqk', qc, k_own).astype(jnp.float32) * scale
        s_own = jnp.where(kpos[None, :] <= qpos[:, None], s_own, -jnp.inf)
        p = jax.nn.softmax(jnp.concatenate([s_sel, s_own], axis=-1), axis=-1)
        p_sel = p[..., :n_sel * MOBA_BLOCK].reshape(b, h, Q_CHUNK, n_sel, MOBA_BLOCK).astype(v.dtype)
        p_own = p[..., n_sel * MOBA_BLOCK:].astype(v.dtype)
        return (jnp.einsum('bhqnl,bhqnld->bhqd', p_sel, vg)
                + jnp.einsum('bhqk,bhkd->bhqd', p_own, v_own))

    out = lax.map(one_chunk, jnp.arange(s // Q_CHUNK))
    return out.transpose(1, 2, 0, 3, 4).reshape(b, h, s, hd)

def setup_inputs(seed: int = 0) -> dict:
    key = jax.random.key(seed)
    ks = jax.random.split(key, 16)
    nrm = lambda k, shape, fan_in: jax.random.normal(k, shape, jnp.float32) * (fan_in ** -0.5)
    return {
        "x": jax.random.normal(ks[0], (BATCH, SEQ, D_MODEL), jnp.float32),
        "norm_mix": 1.0 + 0.02 * jax.random.normal(ks[1], (D_MODEL,), jnp.float32),
        "w_in": nrm(ks[2], (D_MODEL, D_IN), D_MODEL),
        "conv_a_w": nrm(ks[3], (CONV_W, D_CONV), CONV_W),
        "q_norm": 1.0 + 0.02 * jax.random.normal(ks[4], (HEAD_DIM,), jnp.float32),
        "k_norm": 1.0 + 0.02 * jax.random.normal(ks[5], (HEAD_DIM,), jnp.float32),
        "w_out_a": nrm(ks[6], (D_CONV, D_MODEL), D_CONV),
        "w_out_b": nrm(ks[7], (D_ATTN, D_MODEL), D_ATTN),
        "w_o": nrm(ks[8], (D_MODEL, D_MODEL), D_MODEL),
        "norm_ffn": 1.0 + 0.02 * jax.random.normal(ks[9], (D_MODEL,), jnp.float32),
        "w_up": nrm(ks[10], (D_MODEL, 2 * D_FF), D_MODEL),
        "ffn_conv_w": nrm(ks[11], (CONV_W, 2 * D_FF), CONV_W),
        "ffn_conv_b": 0.02 * jax.random.normal(ks[12], (2 * D_FF,), jnp.float32),
        "w_down": nrm(ks[13], (D_FF, D_MODEL), D_FF),
    }

def reference(x, norm_mix, w_in, conv_a_w, q_norm, k_norm, w_out_a, w_out_b, w_o,
              norm_ffn, w_up, ffn_conv_w, ffn_conv_b, w_down):
    b, s, _ = x.shape
    for _layer in range(DEPTH):
        xn = rmsnorm(x, norm_mix)
        z = xn @ w_in
        offs = np.cumsum([0, D_CONV, D_CONV, D_CONV, D_ATTN, D_ATTN, D_ATTN, D_MODEL, D_MODEL])
        bg, cg, xa, q, k, v, ga, gb = [z[..., offs[i]:offs[i + 1]] for i in range(8)]
        branch_a = (bg * causal_dwconv(cg * xa, conv_a_w)) @ w_out_a
        heads = lambda t: t.reshape(b, s, N_HEADS, HEAD_DIM).transpose(0, 2, 1, 3)
        qh = rmsnorm(heads(q), q_norm)
        kh = rmsnorm(heads(k), k_norm)
        o = moba_attention(qh, kh, heads(v))
        branch_b = o.transpose(0, 2, 1, 3).reshape(b, s, D_ATTN) @ w_out_b
        merged = jax.nn.sigmoid(ga) * branch_a + jax.nn.sigmoid(gb) * branch_b
        x = x + merged @ w_o
        hn = rmsnorm(x, norm_ffn)
        u = causal_dwconv(hn @ w_up, ffn_conv_w) + ffn_conv_b
        gate, val = u[..., :D_FF], u[..., D_FF:]
        x = x + (jax.nn.silu(gate) * val) @ w_down
    return x


_drawn_inputs = setup_inputs


def setup_inputs(seed=0):
    import zlib

    import numpy as np

    out = dict(_drawn_inputs(seed))
    spreads = {}
    factors = {'norm_mix': 2.795,
     'q_norm': 8.0,
     'k_norm': 21.909,
     'norm_ffn': 12.246,
     'ffn_conv_b': 12.455}
    for name, (base, spread) in spreads.items():
        noise = np.random.default_rng([zlib.crc32(name.encode()), seed]).standard_normal(out[name].shape)
        drawn = base * np.exp(spread * noise) if base else spread * noise
        out[name] = __import__('jax').numpy.asarray(drawn.astype(out[name].dtype))
    for name, factor in factors.items():
        out[name] = (out[name] * factor).astype(out[name].dtype)
    return out
```

```python
from contextlib import ExitStack

import concourse.bass as bass
from concourse import mybir

F32 = mybir.dt.float32
F32R = mybir.dt.float32r
BF16 = mybir.dt.bfloat16
ALU = mybir.AluOpType
ACT = mybir.ActivationFunctionType
AX_X = mybir.AxisListType.X

P = 128
SEQ = 256
TT = SEQ // P
D = 1024
KT = D // P
HEADS = 8
DFF = 2816
FT = DFF // P
EPS = 1e-6
SCALE = float(P) ** -0.5
MASKED = -3.0e38
UNIT = 2048
SLOTS = 4

SEC_V, SEC_GA, SEC_C, SEC_X, SEC_OUTB, SEC_WO = 2, 3, 5, 6, 8, 10
U_GA, U_C, U_X, U_B, U_OUTB, U_OUTA, U_WO = 12, 20, 24, 28, 32, 36, 40
U_FFN = 44
PAIRS = FT // 2

PC_CONV_A = 0
PC_QN = PC_CONV_A + KT * 3
PC_KN = PC_QN + 1
PC_FW = PC_KN + 1
PC_FB = PC_FW + FT * 2 * 3
PC_NM = PC_FB + FT * 2
PC_ALL = PC_NM + KT


def build(nc, x, norm_ffn, params, stream, out):
    ctx = ExitStack()
    with ctx:
        def sb(name, shape, dt=F32):
            return ctx.enter_context(nc.sbuf_tensor(name, shape, dt))

        def sem(name):
            return ctx.enter_context(nc.semaphore(name))

        raw = sb("raw", [P, SLOTS, UNIT])
        w_hi = sb("w_hi", [P, SLOTS, UNIT], F32R)
        w_lo = sb("w_lo", [P, SLOTS, UNIT], F32R)
        acts = sb("acts", [P, 3, 2, KT, SEQ], F32R)
        x_tok = sb("x_tok", [P, TT, D])
        qkv = sb("qkv", [P, 3, TT, D])
        gates = sb("gates", [P, 2, KT, SEQ])
        prm = sb("prm", [P, PC_ALL])
        ident = sb("ident", [P, P])
        ident_bf = sb("ident_bf", [P, P], BF16)
        mask_bf = sb("mask_bf", [P, P], BF16)
        ones = sb("ones", [P, P])
        diag = sb("diag", [P, TT, P])
        r_row = sb("r_row", [P, SEQ])
        qkT = sb("qkT", [P, 2, 2, SEQ])
        probs = sb("probs", [P, 2, 3, P])
        probsT = sb("probsT", [P, 2, 3, P])
        ssq = sb("ssq", [P, TT, 2, HEADS])
        rqk = sb("rqk", [P, TT, 2, HEADS])
        ssx = sb("ssx", [P, TT])
        ssh = sb("ssh", [P, TT, 2])
        sst = sb("sst", [P, TT])
        rx = sb("rx", [P, TT])
        rh = sb("rh", [P, TT])
        half = sb("half", [P, 2 * TT * HEADS])
        mx = sb("mx", [P, 2, 2])
        negmx = sb("negmx", [P, 2, 2])
        psums = sb("psums", [P, 2, 2])
        rsums = sb("rsums", [P, 2, 2])

        gflat = gates[:].rearrange("p a k t -> p (a k t)")
        qflat = qkv[:].rearrange("p s t d -> p (s t d)")
        sq_tmp = gflat[:, 0:1024].rearrange("p (t d) -> p t d", t=TT)
        junk_x = qflat[:, 0:1024]
        xn_feat = qflat[:, 4096:6144].rearrange("p (k t) -> p k t", k=KT)
        u_feat = qflat[:, 0:2048].rearrange("p (k t) -> p k t", k=KT)
        conv_feat = qflat[:, 2048:4096].rearrange("p (k t) -> p k t", k=KT)
        br_feat = qflat[:, 4096:6144].rearrange("p (k t) -> p k t", k=KT)
        a_feat = br_feat
        hg_tok = qflat[:, 0:2048].rearrange("p (t d) -> p t d", t=TT)
        g_ffn = qflat[:, 2048:3072]
        junk_h = gflat[:, 2048:4096].rearrange("p (t c d) -> p t c d", t=TT, c=2)
        y_up = gflat[:, 0:1024].rearrange("p (u g t) -> p u g t", u=2, g=2)
        silu_g = gflat[:, 1024:1536].rearrange("p (u t) -> p u t", u=2)
        up_sc = qflat[:, 3072:4096].rearrange("p (u g t) -> p u g t", u=2, g=2)
        s_pair = gflat[:, 1536:2048].rearrange("p (u t) -> p u t", u=2)
        out_tok = qflat[:, 4096:6144].rearrange("p (t d) -> p t d", t=TT)

        banks = [ctx.enter_context(nc.psum_tensor(f"bank{i}", [P, 512], F32)) for i in range(8)]
        zb = banks[0:4]
        qkT_ps, score_ps, probsT_ps, o_ps = banks[4:8]
        tb = banks[4:8]
        r_ps = {"x": banks[3], "h": banks[7]}
        upb = banks[4:6]

        x_landed = [sem(f"x_landed{t}") for t in range(TT)]
        gffn_landed, prm_landed = sem("gffn_landed"), sem("prm_landed")
        first_landed = [sem(f"first_landed{c}") for c in range(3)]
        first_hi, first_lo = sem("first_hi"), sem("first_lo")
        raw_landed = [sem(f"raw_landed{s}") for s in range(SLOTS)]
        ffn_landed = [sem(f"ffn_landed{s}") for s in range(SLOTS)]
        out_stored = sem("out_stored")
        hi_ready, lo_ready, weights_used = sem("hi_ready"), sem("lo_ready"), sem("weights_used")
        zeroed, ident_ready, half_ready = sem("zeroed"), sem("ident_ready"), sem("half_ready")
        x_turned, xT_hi, xT_ready = sem("x_turned"), sem("xT_hi"), sem("xT_ready")
        x_squared, x_rms_step, x_rms = sem("x_squared"), sem("x_rms_step"), sem("x_rms")
        xn_ready, xn_hi, xn_split = sem("xn_ready"), sem("xn_hi"), sem("xn_split")
        diag_ready, r_broadcast, r_row_ready = sem("diag_ready"), sem("r_broadcast"), sem("r_row_ready")
        h_added, h_squared, h_rms_step, h_rms = sem("h_added"), sem("h_squared"), sem("h_rms_step"), sem("h_rms")
        hg_ready, h_turned, hT_hi, hT_ready = sem("hg_ready"), sem("h_turned"), sem("hT_hi"), sem("hT_ready")
        qkv_copied, qk_squared, ssq_ready = sem("qkv_copied"), sem("qk_squared"), sem("ssq_ready")
        qk_rms_step, qk_rms = sem("qk_rms_step"), sem("qk_rms")
        qk_normed, qk_turned, qkT_ready = sem("qk_normed"), sem("qk_turned"), sem("qkT_ready")
        scores_ready, max_found, negmax_ready = sem("scores_ready"), sem("max_found"), sem("negmax_ready")
        exp_done, sums_inverted, probs_ready = sem("exp_done"), sem("sums_inverted"), sem("probs_ready")
        probs_turned, probsT_ready, o_ready = sem("probs_turned"), sem("probsT_ready"), sem("o_ready")
        o_hi, branch_split = sem("o_hi"), sem("branch_split")
        gate_copied, feat_taken = sem("gate_copied"), sem("feat_taken")
        gates_ready, conv_step = sem("gates_ready"), sem("conv_step")
        a_hi, m_sum, m_hi, m_ready = sem("a_hi"), sem("m_sum"), sem("m_hi"), sem("m_ready")
        wo_ready = sem("wo_ready")
        up_scaled, up_tap2, up_tap1, up_conv = sem("up_scaled"), sem("up_tap2"), sem("up_tap1"), sem("up_conv")
        silu_ready, s_product, s_hi, s_ready = sem("silu_ready"), sem("s_product"), sem("s_hi"), sem("s_ready")
        down_ready, out_ready = sem("down_ready"), sem("out_ready")

        def bank_pair(b):
            return b[:].rearrange("p (a t) -> p a t", a=2)

        block = ctx.enter_context(nc.Block())

        @block.sync
        def _(sp):
            def unit_at(n):
                return stream[bass.ds(n, 1), :, :].rearrange("a p n -> (a p) n")

            sp.dma_start(prm[:], params).then_inc(prm_landed, 16)
            for t in range(TT):
                sp.dma_start(x_tok[:, t, :], x[t * P:(t + 1) * P, :]).then_inc(x_landed[t], 16)
            for c in range(4):
                part = slice(c * 512, (c + 1) * 512)
                sp.dma_start(raw[:, 0, part], stream[0, :, part]).then_inc((first_landed + [raw_landed[0]])[c], 16)
            for s in range(1, SLOTS):
                sp.dma_start(raw[:, s, :], stream[s, :, :]).then_inc(raw_landed[s], 16)
            with sp.Fori(1, U_FFN // SLOTS) as i:
                for s in range(SLOTS):
                    sp.wait_ge(lo_ready, i * SLOTS + (s + 1 - SLOTS))
                    sp.dma_start(raw[:, s, :], unit_at(i * SLOTS + s)).then_inc(raw_landed[s], 16)
            sp.wait_ge(feat_taken, U_OUTB - U_C)
            sp.dma_start(g_ffn, norm_ffn.to_broadcast([P, D])).then_inc(gffn_landed, 16)

            def load_ffn(slot, unit, split_before):
                sp.wait_ge(lo_ready, split_before)
                sp.dma_start(raw[:, slot, :], unit).then_inc(ffn_landed[slot], 16)

            for slot, pos, before in ((0, 44, 41), (1, 45, 42), (2, 46, 43), (3, 47, 44), (0, 48, 45)):
                load_ffn(slot, stream[pos, :, :], before)
            with sp.Fori(2, PAIRS) as j:
                for n, slot in enumerate((1, 2, 0)):
                    load_ffn(slot, unit_at(j * 3 + (U_FFN - 1 + n)), j * 3 + (U_FFN - 3 + n))
            load_ffn(3, stream[U_FFN + 3 * PAIRS - 1, :, :], 48)
            for t in range(TT):
                sp.wait_ge(out_ready, 2 * (t + 1))
                sp.dma_start(out[t * P:(t + 1) * P, :], out_tok[:, t, :]).then_inc(out_stored, 16)
            sp.wait_ge(out_stored, 16 * TT)

        @block.gpsimd
        def _(pool):
            pool.memset(ident[:], 0.0).then_inc(zeroed, 1)
            pool.memset(ident_bf[:], 0.0).then_inc(zeroed, 1)
            pool.memset(mask_bf[:], 0.0).then_inc(zeroed, 1)
            pool.memset(ones[:], 1.0)
            pool.memset(half[:], -0.5).then_inc(half_ready, 1)
            pool.wait_ge(zeroed, 3)
            for m in (ident, ident_bf):
                pool.affine_select(out=m[:], in_=m[:], compare_op=ALU.not_equal, fill=1.0, base=0,
                                   pattern=[[-1, P]], channel_multiplier=1).then_inc(ident_ready, 1)
            pool.affine_select(out=mask_bf[:], in_=mask_bf[:], compare_op=ALU.is_ge, fill=MASKED, base=0,
                               pattern=[[-1, P]], channel_multiplier=1).then_inc(ident_ready, 1)
            pool.wait_ge(half_ready, 1)
            for t in range(TT):
                pool.wait_ge(x_squared, t + 1)
                pool.tensor_scalar(sst[:, t:t + 1], ssx[:, t:t + 1], 1.0 / D, EPS, ALU.mult, ALU.add).then_inc(x_rms_step, 1)
                pool.wait_ge(x_rms_step, t + 1)
                pool.tensor_tensor(rx[:, t:t + 1], sst[:, t:t + 1], half[:, 0:1], ALU.pow).then_inc(x_rms, 1)
            pool.wait_ge(ssq_ready, 4)
            pool.tensor_scalar(rqk[:], ssq[:], 1.0 / P, EPS, ALU.mult, ALU.add).then_inc(qk_rms_step, 1)
            pool.wait_ge(qk_rms_step, 1)
            pool.tensor_tensor(rqk[:].rearrange("p t s h -> p (t s h)"), rqk[:].rearrange("p t s h -> p (t s h)"),
                               half[:], ALU.pow).then_inc(qk_rms, 1)
            for t in range(TT):
                pool.wait_ge(h_squared, 2 * (t + 1))
                pool.tensor_tensor(rh[:, t:t + 1], ssh[:, t, 0:1], ssh[:, t, 1:2], ALU.add).then_inc(h_rms_step, 1)
                pool.wait_ge(h_rms_step, 2 * t + 1)
                pool.tensor_scalar(sst[:, t:t + 1], rh[:, t:t + 1], 1.0 / D, EPS, ALU.mult, ALU.add).then_inc(h_rms_step, 1)
                pool.wait_ge(h_rms_step, 2 * t + 2)
                pool.tensor_tensor(rh[:, t:t + 1], sst[:, t:t + 1], half[:, 0:1], ALU.pow).then_inc(h_rms, 1)

        @block.scalar
        def _(act):
            def split_hi(slot, landed, count, used=None):
                act.wait_ge(landed[slot], count)
                if used is not None:
                    act.wait_ge(weights_used, used)
                act.activation(w_hi[:, slot, :], raw[:, slot, :], ACT.Copy).then_inc(hi_ready, 1)

            def split_ahead(slot, i):
                split_hi(slot, raw_landed, i * 16 + 16, i * SLOTS + (slot + 1 - SLOTS))

            def split_step(n):
                split_ahead(n % SLOTS, n // SLOTS + 1)

            def xT_hi_part(b):
                act.wait_ge(x_turned, b + 1)
                for k in (2 * b, 2 * b + 1):
                    ins = act.activation(acts[:, 1, 0, k, :], tb[b][:, (k % 2) * SEQ:(k % 2 + 1) * SEQ], ACT.Copy,
                                         scale=prm[:, PC_NM + k:PC_NM + k + 1])
                ins.then_inc(xT_hi, 1)

            def first_hi_part(c):
                part = slice(c * 512, (c + 1) * 512)
                act.wait_ge((first_landed + [raw_landed[0]])[c], 16)
                act.activation(w_hi[:, 0, part], raw[:, 0, part], ACT.Copy).then_inc(first_hi if c < 3 else hi_ready, 1)

            act.wait_ge(prm_landed, 16)
            xT_hi_part(0)
            first_hi_part(0)
            first_hi_part(1)
            xT_hi_part(1)
            first_hi_part(2)
            first_hi_part(3)
            xT_hi_part(2)
            xT_hi_part(3)
            split_hi(1, raw_landed, 16)
            for t in range(TT):
                act.wait_ge(x_landed[t], 16)
                if t:
                    act.wait_ge(x_squared, t)
                act.activation(junk_x, x_tok[:, t, :], ACT.Square, accum_out=ssx[:, t:t + 1]).then_inc(x_squared, 1)
            split_hi(2, raw_landed, 16)
            split_hi(3, raw_landed, 16)
            act.wait_ge(xn_ready, 1)
            act.activation(acts[:, 2, 0, :, :], xn_feat, ACT.Copy).then_inc(xn_hi, 1)

            def qkv_section(i, squares):
                for s in range(SLOTS):
                    if s % 2:
                        c = s // 2
                        act.wait_ge(weights_used, i * SLOTS + (s + 1))
                        for t in range(TT):
                            done = act.activation(qkv[:, bass.ds(i, 1), t, c * 512:(c + 1) * 512].rearrange("p a d -> p (a d)"),
                                                  zb[2 * c + t][:], ACT.Copy, scale=rx[:, t:t + 1])
                            if not squares:
                                done.then_inc(qkv_copied, 1)
                        if squares:
                            for t in range(TT):
                                act.activation(sq_tmp[:, t, :], zb[2 * c + t][:], ACT.Square,
                                               scale=rx[:, t:t + 1]).then_inc(qk_squared, 1)
                    split_ahead(s, i + 1)
                    if s % 2 and squares:
                        act.wait_ge(ssq_ready, i * 2 + (c + 1))

            act.wait_ge(x_rms, TT)
            with act.Fori(0, SEC_V) as i:
                qkv_section(i, True)
            qkv_section(SEC_V, False)

            for u in range(HEADS):
                par = u % 2
                act.wait_ge(qk_turned, u + 1)
                if u >= 2:
                    act.wait_ge(scores_ready, u - 1)
                act.activation(qkT[:, par, 0, :], qkT_ps[:, 0:SEQ], ACT.Copy, scale=prm[:, PC_QN:PC_QN + 1])
                act.activation(qkT[:, par, 1, :], qkT_ps[:, SEQ:2 * SEQ], ACT.Copy,
                               scale=prm[:, PC_KN:PC_KN + 1]).then_inc(qkT_ready, 1)
                n = U_GA + u
                if u:
                    split_step(n - 1)
                act.wait_ge(negmax_ready, u + 1)
                if u >= 2:
                    act.wait_ge(probs_turned, u - 1)
                act.activation(probs[:, par, 0:2, :], score_ps[:, 0:SEQ].rearrange("p (a k) -> p a k", a=2), ACT.Exp,
                               bias=negmx[:, par, 0:1], scale=SCALE, accum_out=psums[:, par, 0:1])
                act.activation(probs[:, par, 2, :], score_ps[:, SEQ:SEQ + P], ACT.Exp,
                               bias=negmx[:, par, 1:2], scale=SCALE, accum_out=psums[:, par, 1:2]).then_inc(exp_done, 1)
                act.wait_ge(weights_used, n + 1)
                act.activation(gates[:, u // 4, 2 * (u % 4):2 * (u % 4) + 2, :], bank_pair(zb[n % 4]),
                               ACT.Copy).then_inc(gate_copied, 1)

            for n in range(U_C, U_B):
                split_step(n - 1)
                if n % 4 == 1:
                    g = (n - U_C) // 4
                    act.wait_ge(gate_copied, 4 * (g + 1))
                    act.activation(gates[:, g, :, :], gates[:, g, :, :], ACT.Sigmoid).then_inc(gates_ready, 1)
            for u in range(4):
                n = U_B + u
                split_step(n - 1)
                act.wait_ge(feat_taken, n + 1 - U_C)
                act.activation(acts[:, 1, 0, 2 * u:2 * u + 2, :], a_feat[:, 2 * u:2 * u + 2, :], ACT.Copy).then_inc(a_hi, 1)
            for n in range(U_OUTB, U_OUTA):
                split_step(n - 1)
            split_step(U_OUTA - 1)
            for u in range(4):
                split_step(U_OUTA + u)
                act.wait_ge(m_sum, u + 1)
                act.activation(acts[:, 2, 0, 2 * u:2 * u + 2, :], br_feat[:, 2 * u:2 * u + 2, :], ACT.Copy).then_inc(m_hi, 1)

            def h_squares(t, c):
                act.wait_ge(h_added, 2 * t + c + 1)
                act.activation(junk_h[:, t, c, :], x_tok[:, t, c * 512:(c + 1) * 512], ACT.Square,
                               accum_out=ssh[:, t, c:c + 1]).then_inc(h_squared, 1)

            def hT_hi_part(b):
                act.wait_ge(h_turned, b + 1)
                t, k4 = b // 2, 4 * (b % 2)
                act.activation(acts[:, 1, 0, k4:k4 + 4, t * P:(t + 1) * P], tb[b][:].rearrange("p (k t) -> p k t", k=4),
                               ACT.Copy).then_inc(hT_hi, 1)

            h_squares(0, 0)
            h_squares(0, 1)
            hT_hi_part(0)
            split_hi(0, ffn_landed, 16, 41)
            hT_hi_part(1)
            h_squares(1, 0)
            split_hi(1, ffn_landed, 16, 42)
            hT_hi_part(2)
            hT_hi_part(3)
            h_squares(1, 1)
            split_hi(2, ffn_landed, 16, 43)
            split_hi(3, ffn_landed, 16, 44)

            def tap2(u, j):
                act.wait_ge(up_scaled, j * 2 + (u + 1))
                if not (isinstance(j, int) and j == 0):
                    act.wait_ge(s_product, j * 2 + (u - 1))
                for g in range(2):
                    col = j * 4 + (2 * u + g)
                    ins = act.activation(y_up[:, u, g, :], up_sc[:, u, g, :], ACT.Identity,
                                         scale=prm[:, bass.ds(col * 3 + (PC_FW + 2), 1)],
                                         bias=prm[:, bass.ds(col + PC_FB, 1)])
                ins.then_inc(up_tap2, 1)

            def silu(u, j):
                act.wait_ge(up_conv, j * 2 + (u + 1))
                act.activation(silu_g[:, u, :], y_up[:, u, 0, :], ACT.Silu).then_inc(silu_ready, 1)

            def hidden_hi(j, used, region=0):
                act.wait_ge(s_product, j * 2 + 2)
                if used is not None:
                    act.wait_ge(weights_used, used)
                act.activation(acts[:, region, 0, 0:2, :], s_pair, ACT.Copy).then_inc(s_hi, 1)

            tap2(0, 0)
            split_hi(0, ffn_landed, 32, 45)
            silu(0, 0)
            tap2(1, 0)
            split_hi(1, ffn_landed, 32, 46)
            silu(1, 0)
            hidden_hi(0, None)
            tap2(0, 1)
            split_hi(2, ffn_landed, 32, 47)
            silu(0, 1)
            tap2(1, 1)
            silu(1, 1)
            hidden_hi(1, 49)
            with act.Fori(2, PAIRS - 1) as j:
                split_hi(0, ffn_landed, j * 16 + 16, j * 3 + (U_FFN - 1))
                tap2(0, j)
                split_hi(1, ffn_landed, j * 16 + 16, j * 3 + U_FFN)
                silu(0, j)
                tap2(1, j)
                split_hi(2, ffn_landed, j * 16 + 16, j * 3 + (U_FFN + 1))
                silu(1, j)
                hidden_hi(j, j * 3 + (U_FFN + 2))
            j = PAIRS - 1
            split_hi(0, ffn_landed, j * 16 + 16, j * 3 + (U_FFN - 1))
            tap2(0, j)
            split_hi(3, ffn_landed, 32)
            silu(0, j)
            tap2(1, j)
            silu(1, j)
            hidden_hi(j, None, region=2)

        @block.vector
        def _(dve):
            def split_lo(slot, count):
                dve.wait_ge(hi_ready, count)
                dve.tensor_tensor(w_lo[:, slot, :], raw[:, slot, :], w_hi[:, slot, :].bitcast(F32),
                                  ALU.subtract).then_inc(lo_ready, 1)

            def xT_lo_part(b):
                dve.wait_ge(xT_hi, b + 1)
                for k in (2 * b, 2 * b + 1):
                    ins = dve.scalar_tensor_tensor(out=acts[:, 1, 1, k, :], in0=tb[b][:, (k % 2) * SEQ:(k % 2 + 1) * SEQ],
                                                   scalar=prm[:, PC_NM + k:PC_NM + k + 1],
                                                   in1=acts[:, 1, 0, k, :].bitcast(F32), op0=ALU.mult, op1=ALU.subtract)
                ins.then_inc(xT_ready, 1)

            def first_lo_part(c):
                part = slice(c * 512, (c + 1) * 512)
                if c < 3:
                    dve.wait_ge(first_hi, c + 1)
                else:
                    dve.wait_ge(hi_ready, 1)
                dve.tensor_tensor(w_lo[:, 0, part], raw[:, 0, part], w_hi[:, 0, part].bitcast(F32),
                                  ALU.subtract).then_inc(first_lo if c < 3 else lo_ready, 1)

            def broadcast_rms(r, rms):
                dve.wait_ge(rms, TT)
                for t in range(TT):
                    ins = dve.tensor_scalar(diag[:, t, :], ident[:], r[:, t:t + 1], None, ALU.mult)
                ins.then_inc(diag_ready, 1)

            def take_r_row(which, count):
                dve.wait_ge(r_broadcast, count)
                dve.tensor_copy(r_row[:], r_ps[which][:, 0:SEQ]).then_inc(r_row_ready, 1)
                dve.wait_ge(r_row_ready, count)

            dve.wait_ge(prm_landed, 16)
            dve.wait_ge(ident_ready, 3)
            xT_lo_part(0)
            first_lo_part(0)
            first_lo_part(1)
            xT_lo_part(1)
            first_lo_part(2)
            first_lo_part(3)
            xT_lo_part(2)
            xT_lo_part(3)
            split_lo(1, 2)
            broadcast_rms(rx, x_rms)
            split_lo(2, 3)
            take_r_row("x", 1)
            for k in range(KT):
                ins = dve.scalar_tensor_tensor(out=xn_feat[:, k, :], in0=tb[k // 2][:, (k % 2) * SEQ:(k % 2 + 1) * SEQ],
                                               scalar=prm[:, PC_NM + k:PC_NM + k + 1], in1=r_row[:], op0=ALU.mult, op1=ALU.mult)
            ins.then_inc(xn_ready, 1)
            split_lo(3, 4)
            dve.wait_ge(xn_hi, 1)
            dve.tensor_tensor(acts[:, 2, 1, :, :], xn_feat, acts[:, 2, 0, :, :].bitcast(F32), ALU.subtract).then_inc(xn_split, 1)

            def qkv_section(i, squares):
                for s in range(SLOTS):
                    if squares and s % 2:
                        c = s // 2
                        dve.wait_ge(qk_squared, i * 4 + (2 * c + 2))
                        dve.tensor_reduce(ssq[:, :, bass.ds(i, 1), 4 * c:4 * c + 4].rearrange("p t s h -> p t (s h)"),
                                          sq_tmp[:].rearrange("p t (h d) -> p t h d", h=4),
                                          axis=AX_X, op=ALU.add).then_inc(ssq_ready, 1)
                    if not squares and s == 0:
                        norm_qk(0)
                    split_lo(s, i * SLOTS + (s + 5))

            def norm_qk(h):
                for t in range(TT):
                    view = qkv[:, 0:2, t, h * P:(h + 1) * P]
                    ins = dve.tensor_tensor(view, view, rqk[:, t, :, h:h + 1].to_broadcast([P, 2, P]), ALU.mult)
                ins.then_inc(qk_normed, 1)

            with dve.Fori(0, SEC_V) as i:
                qkv_section(i, True)
            dve.wait_ge(qk_rms, 1)
            qkv_section(SEC_V, False)

            def attention_tail(h):
                par = h % 2
                dve.wait_ge(probs_turned, h + 1)
                if h >= 2:
                    dve.wait_ge(o_ready, h - 1)
                dve.tensor_copy(probsT[:, par, :, :], probsT_ps[:, 0:3 * P].rearrange("p (a q) -> p a q", a=3)).then_inc(probsT_ready, 1)

            def attention_out(h):
                dve.wait_ge(o_ready, h + 1)
                dve.tensor_copy(acts[:, 0, 0, h, :], o_ps[:, 0:SEQ]).then_inc(o_hi, 1)
                dve.wait_ge(o_hi, h + 1)
                dve.tensor_tensor(acts[:, 0, 1, h, :], o_ps[:, 0:SEQ], acts[:, 0, 0, h, :].bitcast(F32),
                                  ALU.subtract).then_inc(branch_split, 1)

            for u in range(HEADS):
                par = u % 2
                n = U_GA + u
                if u + 1 < HEADS:
                    norm_qk(u + 1)
                if u:
                    split_lo((n + 3) % SLOTS, n + 4)
                dve.wait_ge(scores_ready, u + 1)
                dve.reduce_max(mx[:, par, 0:1], score_ps[:, 0:SEQ], AX_X)
                dve.reduce_max(mx[:, par, 1:2], score_ps[:, SEQ:SEQ + P], AX_X).then_inc(max_found, 1)
                dve.wait_ge(max_found, u + 1)
                dve.tensor_scalar(negmx[:, par, :], mx[:, par, :], -SCALE, None, ALU.mult).then_inc(negmax_ready, 1)
                if u:
                    attention_tail(u - 1)
                dve.wait_ge(exp_done, u + 1)
                dve.reciprocal(rsums[:, par, :], psums[:, par, :]).then_inc(sums_inverted, 1)
                dve.wait_ge(sums_inverted, u + 1)
                dve.tensor_scalar(probs[:, par, 0:2, :], probs[:, par, 0:2, :], rsums[:, par, 0:1], None, ALU.mult)
                dve.tensor_scalar(probs[:, par, 2, :], probs[:, par, 2, :], rsums[:, par, 1:2], None,
                                  ALU.mult).then_inc(probs_ready, 1)
                if u:
                    attention_out(u - 1)

            for u in range(4):
                n = U_C + u
                split_lo((n + 3) % SLOTS, n + 4)
                if u == 0:
                    attention_tail(HEADS - 1)
                dve.wait_ge(weights_used, n + 1)
                dve.tensor_copy(u_feat[:, 2 * u:2 * u + 2, :], bank_pair(zb[n % 4])).then_inc(feat_taken, 1)
                if u == 0:
                    attention_out(HEADS - 1)
            dve.wait_ge(prm_landed, 16)
            for u in range(4):
                n = U_X + u
                split_lo((n + 3) % SLOTS, n + 4)
                two = slice(2 * u, 2 * u + 2)
                dve.wait_ge(weights_used, n + 1)
                if u == 0:
                    dve.wait_ge(feat_taken, 4)
                dve.tensor_tensor(u_feat[:, two, :], bank_pair(zb[n % 4]), u_feat[:, two, :], ALU.mult).then_inc(feat_taken, 1)
                dve.wait_ge(feat_taken, 5 + u)
                for tap in (2, 1, 0):
                    shift = 2 - tap
                    for k in (2 * u, 2 * u + 1):
                        w = prm[:, PC_CONV_A + 3 * k + tap:PC_CONV_A + 3 * k + tap + 1]
                        if tap == 2:
                            ins = dve.tensor_scalar(conv_feat[:, k, :], u_feat[:, k, :], w, None, ALU.mult)
                        else:
                            ins = dve.scalar_tensor_tensor(out=conv_feat[:, k, shift:SEQ], in0=u_feat[:, k, 0:SEQ - shift],
                                                           scalar=w, in1=conv_feat[:, k, shift:SEQ], op0=ALU.mult, op1=ALU.add)
                    ins.then_inc(conv_step, 1)
                    dve.wait_ge(conv_step, 3 * u + 3 - tap)
            def a_lo(u):
                two = slice(2 * u, 2 * u + 2)
                dve.wait_ge(a_hi, u + 1)
                ins = dve.tensor_tensor(acts[:, 1, 1, two, :], a_feat[:, two, :], acts[:, 1, 0, two, :].bitcast(F32), ALU.subtract)
                ins.then_inc(branch_split, 1)

            for u in range(4):
                n = U_B + u
                two = slice(2 * u, 2 * u + 2)
                split_lo((n + 3) % SLOTS, n + 4)
                dve.wait_ge(weights_used, n + 1)
                dve.tensor_tensor(a_feat[:, two, :], bank_pair(zb[n % 4]), conv_feat[:, two, :], ALU.mult).then_inc(feat_taken, 1)
                a_lo(u)
            for u in range(4):
                n = U_OUTB + u
                two = slice(2 * u, 2 * u + 2)
                split_lo((n + 3) % SLOTS, n + 4)
                dve.wait_ge(weights_used, n + 1)
                if u == 0:
                    dve.wait_ge(gates_ready, 2)
                dve.tensor_tensor(br_feat[:, two, :], bank_pair(zb[n % 4]), gates[:, 1, two, :], ALU.mult).then_inc(feat_taken, 1)
            split_lo((U_OUTA + 3) % SLOTS, U_OUTA + 4)
            for u in range(4):
                n = U_OUTA + u
                two = slice(2 * u, 2 * u + 2)
                dve.wait_ge(weights_used, n + 1)
                dve.tensor_tensor(u_feat[:, two, :], bank_pair(zb[n % 4]), gates[:, 0, two, :], ALU.mult).then_inc(feat_taken, 1)
                dve.wait_ge(feat_taken, n + 1 - U_C)
                dve.tensor_tensor(br_feat[:, two, :], u_feat[:, two, :], br_feat[:, two, :], ALU.add).then_inc(m_sum, 1)
                if u < 3:
                    split_lo(n % SLOTS, n + 5)
                dve.wait_ge(m_hi, u + 1)
                dve.tensor_tensor(acts[:, 2, 1, two, :], br_feat[:, two, :], acts[:, 2, 0, two, :].bitcast(F32),
                                  ALU.subtract).then_inc(m_ready, 1)
            split_lo(3, U_WO + 4)

            def add_h(t, c):
                if t == 0:
                    dve.wait_ge(wo_ready, c + 1)
                else:
                    dve.wait_ge(weights_used, U_WO + 2 * (c + 1))
                part = x_tok[:, t, c * 512:(c + 1) * 512]
                dve.tensor_tensor(part, zb[2 * t + c][:], part, ALU.add).then_inc(h_added, 1)
                dve.wait_ge(h_added, 2 * t + c + 1)
                dve.tensor_tensor(hg_tok[:, t, c * 512:(c + 1) * 512], part, g_ffn[:, c * 512:(c + 1) * 512],
                                  ALU.mult).then_inc(hg_ready, 1)

            def hT_lo_part(b):
                dve.wait_ge(hT_hi, b + 1)
                t, k4 = b // 2, 4 * (b % 2)
                dve.tensor_tensor(acts[:, 1, 1, k4:k4 + 4, t * P:(t + 1) * P], tb[b][:].rearrange("p (k t) -> p k t", k=4),
                                  acts[:, 1, 0, k4:k4 + 4, t * P:(t + 1) * P].bitcast(F32), ALU.subtract).then_inc(hT_ready, 1)

            dve.wait_ge(gffn_landed, 16)
            add_h(0, 0)
            add_h(0, 1)
            hT_lo_part(0)
            add_h(1, 0)
            split_lo(0, U_FFN + 1)
            hT_lo_part(1)
            add_h(1, 1)
            hT_lo_part(2)
            hT_lo_part(3)
            split_lo(1, U_FFN + 2)
            broadcast_rms(rh, h_rms)
            split_lo(2, U_FFN + 3)
            split_lo(3, U_FFN + 4)
            take_r_row("h", 2)

            def scale_up(u, j):
                first = isinstance(j, int) and j == 0
                dve.wait_ge(weights_used, U_FFN + 1 + u if first else j * 3 + (U_FFN + u))
                dve.tensor_tensor(up_sc[:, u, :, :], bank_pair(upb[u]), r_row[:].unsqueeze(1).to_broadcast([P, 2, SEQ]),
                                  ALU.mult).then_inc(up_scaled, 1)

            def taps(u, j):
                dve.wait_ge(up_tap2, j * 2 + (u + 1))
                for tap, signal in ((1, up_tap1), (0, up_conv)):
                    shift = 2 - tap
                    for g in range(2):
                        y = y_up[:, u, g, shift:SEQ]
                        w = prm[:, bass.ds((j * 4 + (2 * u + g)) * 3 + (PC_FW + tap), 1)]
                        ins = dve.scalar_tensor_tensor(out=y, in0=up_sc[:, u, g, 0:SEQ - shift], scalar=w, in1=y,
                                                       op0=ALU.mult, op1=ALU.add)
                    ins.then_inc(signal, 1)
                    if tap:
                        dve.wait_ge(up_tap1, j * 2 + (u + 1))

            def hidden(u, j):
                dve.wait_ge(silu_ready, j * 2 + (u + 1))
                dve.tensor_tensor(s_pair[:, u, :], silu_g[:, u, :], y_up[:, u, 1, :], ALU.mult).then_inc(s_product, 1)

            def hidden_lo(j, region=0):
                dve.wait_ge(s_hi, j + 1)
                dve.tensor_tensor(acts[:, region, 1, 0:2, :], s_pair, acts[:, region, 0, 0:2, :].bitcast(F32),
                                  ALU.subtract).then_inc(s_ready, 1)

            scale_up(0, 0)
            taps(0, 0)
            split_lo(0, 49)
            hidden(0, 0)
            scale_up(1, 0)
            taps(1, 0)
            split_lo(1, 50)
            hidden(1, 0)
            hidden_lo(0)
            scale_up(0, 1)
            taps(0, 1)
            split_lo(2, 51)
            hidden(0, 1)
            scale_up(1, 1)
            taps(1, 1)
            hidden(1, 1)
            hidden_lo(1)
            with dve.Fori(2, PAIRS - 1) as j:
                split_lo(0, j * 3 + (U_FFN + 2))
                scale_up(0, j)
                taps(0, j)
                split_lo(1, j * 3 + (U_FFN + 3))
                hidden(0, j)
                scale_up(1, j)
                taps(1, j)
                split_lo(2, j * 3 + (U_FFN + 4))
                hidden(1, j)
                hidden_lo(j)
            j = PAIRS - 1
            split_lo(0, j * 3 + (U_FFN + 2))
            scale_up(0, j)
            taps(0, j)
            split_lo(3, j * 3 + (U_FFN + 3))
            hidden(0, j)
            scale_up(1, j)
            taps(1, j)
            hidden(1, j)
            hidden_lo(j, region=2)
            for t in range(TT):
                for c in range(2):
                    part = slice(c * 512, (c + 1) * 512)
                    dve.wait_ge(down_ready, 2 * t + c + 1)
                    dve.tensor_tensor(out_tok[:, t, part], zb[2 * t + c][:], x_tok[:, t, part], ALU.add).then_inc(out_ready, 1)

        @block.tensor
        def _(pe):
            def three_pass(out_, st, mv, start, stop):
                pe.matmul(out_, st(0), mv(0), start=start, stop=False)
                pe.matmul(out_, st(0), mv(1), start=False, stop=False)
                return pe.matmul(out_, st(1), mv(0), start=False, stop=stop)

            def weights(part, slot):
                return (w_hi, w_lo)[part][:, slot, :]

            def feature_tile(slot, a, bank, region):
                for k in range(KT):
                    last = three_pass(
                        bank[:, a * SEQ:(a + 1) * SEQ],
                        lambda h: weights(h, slot)[:, k * 256 + a * P:k * 256 + (a + 1) * P],
                        lambda h: acts[:, region, h, k, :] if isinstance(region, int) else
                        acts[:, bass.ds(region, 1), h, k, :].rearrange("p a t -> p (a t)"),
                        k == 0, k == KT - 1)
                return last

            def token_product(slot, k, t, bank, region):
                return three_pass(bank[:], lambda h: acts[:, region, h, k, t * P:(t + 1) * P],
                                  lambda h: weights(h, slot)[:, (k % 4) * 512:(k % 4 + 1) * 512], k == 0, k == KT - 1)

            def broadcast(which, count):
                pe.wait_ge(diag_ready, count)
                for t in range(TT):
                    ins = pe.matmul(r_ps[which][:, t * P:(t + 1) * P], ones[:], diag[:, t, :], start=True, stop=True)
                ins.then_inc(r_broadcast, 1)

            pe.wait_ge(ident_ready, 3)
            for t in range(TT):
                pe.wait_ge(x_landed[t], 16)
                for k in range(KT):
                    ins = pe.transpose(tb[k // 2][:, (k % 2) * SEQ + t * P:(k % 2) * SEQ + (t + 1) * P],
                                       x_tok[:, t, k * P:(k + 1) * P], ident[:])
                    if t == TT - 1 and k % 2:
                        ins.then_inc(x_turned, 1)

            def qkv_section(i, first):
                for c in range(2):
                    if not first:
                        pe.wait_ge(qk_squared, i * 4 + (2 * c - 2))
                    elif c:
                        pe.wait_ge(r_row_ready, 1)
                    for kh in range(2):
                        slot = 2 * c + kh
                        if not first or slot:
                            pe.wait_ge(lo_ready, i * SLOTS + (slot + 1))
                        for k in range(4 * kh, 4 * kh + 4):
                            if first and slot == 0:
                                pe.wait_ge(first_lo if k < 3 else lo_ready, k + 1 if k < 3 else 1)
                            if first and c == 0 and k % 2 == 0:
                                pe.wait_ge(xT_ready, k // 2 + 1)
                            for t in range(TT):
                                last = token_product(slot, k, t, zb[2 * c + t], 1)
                        last.then_inc(weights_used, 1)
                        if first and slot == 0:
                            broadcast("x", 1)

            qkv_section(0, True)
            with pe.Fori(1, SEC_V + 1) as i:
                qkv_section(i, False)
            pe.wait_ge(xn_split, 1)

            def turn_qk(h):
                pe.wait_ge(qk_normed, h + 1)
                if h:
                    pe.wait_ge(qkT_ready, h)
                for s in range(2):
                    for t in range(TT):
                        last = pe.transpose(qkT_ps[:, s * SEQ + t * P:s * SEQ + (t + 1) * P],
                                            qkv[:, s, t, h * P:(h + 1) * P], ident[:])
                last.then_inc(qk_turned, 1)

            def scores(h):
                pe.wait_ge(qkT_ready, h + 1)
                if h:
                    pe.wait_ge(exp_done, h)
                q, k = qkT[:, h % 2, 0, :], qkT[:, h % 2, 1, :]
                pe.matmul(score_ps[:, 0:SEQ], q[:, P:SEQ], k, start=True, stop=False)
                pe.matmul(score_ps[:, P:SEQ], ident_bf[:], mask_bf[:], start=False, stop=True)
                pe.matmul(score_ps[:, SEQ:SEQ + P], q[:, 0:P], k[:, 0:P], start=True, stop=False)
                pe.matmul(score_ps[:, SEQ:SEQ + P], ident_bf[:], mask_bf[:], start=False, stop=True).then_inc(scores_ready, 1)

            def turn_probs(h):
                pe.wait_ge(probs_ready, h + 1)
                if h:
                    pe.wait_ge(probsT_ready, h)
                for src, dst in ((2, 0), (0, 1), (1, 2)):
                    last = pe.transpose(probsT_ps[:, dst * P:(dst + 1) * P], probs[:, h % 2, src, :], ident[:])
                last.then_inc(probs_turned, 1)

            def weigh_values(h):
                pe.wait_ge(probsT_ready, h + 1)
                if h:
                    pe.wait_ge(branch_split, h)
                pT = probsT[:, h % 2, :, :].rearrange("p a q -> p (a q)")
                pe.matmul(o_ps[:, 0:SEQ], qkv[:, 2, 0, h * P:(h + 1) * P], pT[:, 0:SEQ], start=True, stop=False)
                pe.matmul(o_ps[:, P:SEQ], qkv[:, 2, 1, h * P:(h + 1) * P], pT[:, SEQ:SEQ + P], start=False,
                          stop=True).then_inc(o_ready, 1)

            for u in range(U_X - U_GA):
                n = U_GA + u
                slot = n % SLOTS
                if u < HEADS:
                    turn_qk(u)
                pe.wait_ge(lo_ready, n + 1)
                if u < 4:
                    pe.wait_ge(qkv_copied, 2 * (u // 2) + 2)
                else:
                    pe.wait_ge(gate_copied, u - 3)
                feature_tile(slot, 0, zb[slot], 2)
                if u < HEADS:
                    scores(u)
                if 0 < u <= HEADS:
                    turn_probs(u - 1)
                feature_tile(slot, 1, zb[slot], 2).then_inc(weights_used, 1)
                if 0 < u <= HEADS:
                    weigh_values(u - 1)

            def feature_section(i, first_unit, region):
                for s in range(SLOTS):
                    pe.wait_ge(lo_ready, i * SLOTS + (first_unit + s + 1))
                    pe.wait_ge(feat_taken, i * SLOTS + (first_unit + s + 1 - U_X))
                    feature_tile(s, 0, zb[s], region)
                    feature_tile(s, 1, zb[s], region).then_inc(weights_used, 1)

            with pe.Fori(0, 2) as i:
                feature_section(i, U_X, 2)
            with pe.Fori(0, 2) as i:
                pe.wait_ge(branch_split, i * 4 + HEADS)
                feature_section(i, U_OUTB, i)

            def turn_h(t, c):
                b = 2 * t + c
                pe.wait_ge(hg_ready, b + 1)
                for k in range(4):
                    ins = pe.transpose(tb[b][:, k * P:(k + 1) * P], hg_tok[:, t, (4 * c + k) * P:(4 * c + k + 1) * P], ident[:])
                ins.then_inc(h_turned, 1)

            for t in range(TT):
                for c in range(2):
                    if t == 0:
                        pe.wait_ge(feat_taken, U_OUTA - U_C + c + 1)
                    for k in range(KT):
                        if t == 0 and k % 4 == 0:
                            pe.wait_ge(lo_ready, U_WO + 2 * c + k // 4 + 1)
                        if t == 0 and c == 0 and k % 2 == 0:
                            pe.wait_ge(m_ready, k // 2 + 1)
                        last = token_product(2 * c + k // 4, k, t, zb[2 * t + c], 2)
                    if t == 0:
                        last.then_inc(wo_ready, 1)
                    else:
                        last.then_inc(weights_used, 2)
                    if (t, c) == (0, 1):
                        turn_h(0, 0)
                    elif (t, c) == (1, 0):
                        turn_h(0, 1)
            turn_h(1, 0)
            turn_h(1, 1)

            def up(u, slot, split, scaled):
                pe.wait_ge(lo_ready, split)
                if scaled is not None:
                    pe.wait_ge(up_scaled, scaled)
                feature_tile(slot, 0, upb[u], 1)
                feature_tile(slot, 1, upb[u], 1).then_inc(weights_used, 1)

            def down(slot, split, pairs, region=0, start=False, stop=False):
                pe.wait_ge(lo_ready, split)
                pe.wait_ge(s_ready, pairs)
                for t in range(TT):
                    for c in range(2):
                        for kk in range(2):
                            last = three_pass(
                                zb[2 * t + c][:],
                                lambda h: acts[:, region, h, kk, t * P:(t + 1) * P],
                                lambda h: weights(h, slot)[:, kk * D + c * 512:kk * D + (c + 1) * 512],
                                start and kk == 0, stop and kk == 1)
                        if stop:
                            last.then_inc(down_ready, 1)
                if not stop:
                    last.then_inc(weights_used, 1)

            pe.wait_ge(hT_ready, 4)
            up(0, 0, 45, None)
            broadcast("h", 2)
            up(1, 1, 46, None)
            up(0, 2, 47, 1)
            up(1, 3, 48, 2)
            pe.wait_ge(h_added, 4)
            down(0, 49, 1, start=True)
            with pe.Fori(2, PAIRS) as j:
                up(0, 1, j * 3 + U_FFN, j * 2 - 1)
                up(1, 2, j * 3 + (U_FFN + 1), j * 2)
                down(0, j * 3 + (U_FFN + 2), j)
            down(3, 77, PAIRS, region=2, stop=True)


def weight_stream(w_in, w_out_a, w_out_b, w_o, w_up, w_down):
    import numpy as np

    def token(w):
        return w.reshape(2, 4, P, 2, 512).transpose(3, 0, 2, 1, 4).reshape(4, P, UNIT)

    def feature(w):
        return w.reshape(KT, P, 4, 256).transpose(2, 1, 0, 3).reshape(4, P, UNIT)

    b, c, x, q, k, v, ga, gb = (w_in[:, i * D:(i + 1) * D] for i in range(8))
    up = w_up.reshape(KT, P, 2, FT, P).transpose(3, 1, 0, 2, 4).reshape(FT, P, UNIT)
    down = w_down.reshape(PAIRS, 2, P, D).transpose(0, 2, 1, 3).reshape(PAIRS, P, UNIT)
    parts = [token(w) for w in (q, k, v)] + [feature(w) for w in (ga, gb, c, x, b, w_out_b, w_out_a)] + [token(w_o)]
    parts.append(up[0:2])
    for j in range(1, PAIRS):
        parts += [up[2 * j:2 * j + 2], down[j - 1:j]]
    parts.append(down[PAIRS - 1:PAIRS])
    return np.concatenate(parts, axis=0)


def kernel(**inputs):
    import numpy as np
    import concourse.bacc as bacc
    from concourse import mybir as mb
    from concourse.bass_utils import run_bass_kernel_spmd

    a = {k: np.asarray(v) for k, v in inputs.items()}

    def columns(v, tiles):
        return v.reshape(tiles, P).T

    fw = a["ffn_conv_w"].reshape(3, 2, FT, P).transpose(3, 2, 1, 0).reshape(P, FT * 6)
    fb = a["ffn_conv_b"].reshape(2, FT, P).transpose(2, 1, 0).reshape(P, FT * 2)
    arrays = {
        "x": np.ascontiguousarray(a["x"][0]),
        "norm_ffn": a["norm_ffn"].reshape(1, D),
        "params": np.concatenate([a["conv_a_w"].reshape(3, KT, P).transpose(2, 1, 0).reshape(P, KT * 3),
                                  columns(a["q_norm"], 1), columns(a["k_norm"], 1), fw, fb,
                                  columns(a["norm_mix"], KT)], axis=1),
        "stream": weight_stream(a["w_in"], a["w_out_a"], a["w_out_b"], a["w_o"], a["w_up"], a["w_down"]),
    }
    nc = bacc.Bacc("TRN2", target_bir_lowering=False, num_devices=1)
    args = [nc.dram_tensor(n, v.shape, mb.dt.from_np(v.dtype), kind="ExternalInput").ap() for n, v in arrays.items()]
    args.append(nc.dram_tensor("out", (SEQ, D), F32, kind="ExternalOutput").ap())
    build(nc, *args)
    r = run_bass_kernel_spmd(nc, [arrays], core_ids=[0])
    return r.results[0]["out"].reshape(1, SEQ, D)
```

```python
from contextlib import ExitStack

import concourse.bass as bass
from concourse import mybir

F32 = mybir.dt.float32
F32R = mybir.dt.float32r
BF16 = mybir.dt.bfloat16
ALU = mybir.AluOpType
ACT = mybir.ActivationFunctionType
AX_X = mybir.AxisListType.X

P = 128
SEQ = 256
TT = SEQ // P
D = 1024
KT = D // P
HEADS = 8
DFF = 2816
FT = DFF // P
EPS = 1e-6
SCALE = float(P) ** -0.5
MASKED = -3.0e38
UNIT = 2048
SLOTS = 4
WARM_UPS = (7, 3)
QUARTERS = 12

SEC_V = 2
U_GA, U_C, U_X, U_B, U_OUTB, U_OUTA, U_WO = 12, 20, 24, 28, 32, 36, 40
U_FFN = 44
PAIRS = FT // 2
HALF = D // 2
OUT_PARTS = [(t, c) for t in range(TT) for c in range(2)]

PC_CONV_A = 0
PC_QN = PC_CONV_A + KT * 3
PC_KN = PC_QN + 1
PC_FW = PC_KN + 1
PC_FB = PC_FW + FT * 2 * 3
PC_NM = PC_FB + FT * 2
PC_ALL = PC_NM + KT


def build(nc, x, norm_ffn, params, stream, out):
    ctx = ExitStack()
    with ctx:
        def sb(name, shape, dt=F32):
            return ctx.enter_context(nc.sbuf_tensor(name, shape, dt))

        def sem(name):
            return ctx.enter_context(nc.semaphore(name))

        raw = sb("raw", [P, SLOTS, UNIT])
        w_hi = sb("w_hi", [P, SLOTS, UNIT], F32R)
        w_lo = sb("w_lo", [P, SLOTS, UNIT], F32R)
        acts = sb("acts", [P, 3, 2, KT, SEQ], F32R)
        x_tok = sb("x_tok", [P, TT, D])
        qkv = sb("qkv", [P, 3, TT, D])
        gates = sb("gates", [P, 2, KT, SEQ])
        prm = sb("prm", [P, PC_ALL])
        ident = sb("ident", [P, P])
        ident_bf = sb("ident_bf", [P, P], BF16)
        mask_bf = sb("mask_bf", [P, P], BF16)
        ones = sb("ones", [P, P])
        diag = sb("diag", [P, TT, P])
        r_row = sb("r_row", [P, SEQ])
        qkT = sb("qkT", [P, 2, 2, SEQ])
        probs = sb("probs", [P, 2, 3, P])
        probsT = sb("probsT", [P, 2, 3, P])
        ssq = sb("ssq", [P, TT, 2, HEADS])
        rqk = sb("rqk", [P, TT, 2, HEADS])
        ssx = sb("ssx", [P, TT])
        ssh = sb("ssh", [P, TT, 2])
        sst = sb("sst", [P, TT])
        rx = sb("rx", [P, TT])
        rh = sb("rh", [P, TT])
        half = sb("half", [P, 2 * TT * HEADS])
        mx = sb("mx", [P, 2, 2])
        negmx = sb("negmx", [P, 2, 2])
        psums = sb("psums", [P, 2, 2])
        rsums = sb("rsums", [P, 2, 2])

        gflat = gates[:].rearrange("p a k t -> p (a k t)")
        qflat = qkv[:].rearrange("p s t d -> p (s t d)")
        sq_tmp = gflat[:, 0:1024].rearrange("p (t d) -> p t d", t=TT)
        junk_x = qflat[:, 0:1024]
        xn_feat = qflat[:, 4096:6144].rearrange("p (k t) -> p k t", k=KT)
        u_feat = qflat[:, 0:2048].rearrange("p (k t) -> p k t", k=KT)
        conv_feat = qflat[:, 2048:4096].rearrange("p (k t) -> p k t", k=KT)
        br_feat = qflat[:, 4096:6144].rearrange("p (k t) -> p k t", k=KT)
        a_feat = br_feat
        hg_tok = qflat[:, 0:2048].rearrange("p (t d) -> p t d", t=TT)
        g_ffn = qflat[:, 2048:3072]
        junk_h = gflat[:, 2048:4096].rearrange("p (t c d) -> p t c d", t=TT, c=2)
        y_up = gflat[:, 0:1024].rearrange("p (u g t) -> p u g t", u=2, g=2)
        silu_g = gflat[:, 1024:1536].rearrange("p (u t) -> p u t", u=2)
        up_sc = qflat[:, 3072:4096].rearrange("p (u g t) -> p u g t", u=2, g=2)
        s_pair = gflat[:, 1536:2048].rearrange("p (u t) -> p u t", u=2)
        out_tok = qflat[:, 4096:6144].rearrange("p (t d) -> p t d", t=TT)

        banks = [ctx.enter_context(nc.psum_tensor(f"bank{i}", [P, 512], F32)) for i in range(8)]
        zb = banks[0:4]
        qkT_ps, score_ps, probsT_ps, o_ps = banks[4:8]
        tb = banks[4:8]
        r_ps = {"x": banks[3], "h": banks[7]}
        upb = banks[4:6]

        x_landed = [[sem(f"x_landed{t}_{c}") for c in range(2)] for t in range(TT)]
        gffn_landed, prm_landed = sem("gffn_landed"), sem("prm_landed")
        raw_landed = [sem(f"raw_landed{s}") for s in range(SLOTS)]
        quarter_landed = [raw_landed[q // 4] if q % 4 == 3 else sem(f"quarter_landed{q}") for q in range(QUARTERS)]
        quarter_hi, quarter_lo = sem("quarter_hi"), sem("quarter_lo")
        ffn_landed = [sem(f"ffn_landed{s}") for s in range(SLOTS)]
        out_stored = sem("out_stored")
        hi_ready, lo_ready, weights_used = sem("hi_ready"), sem("lo_ready"), sem("weights_used")
        zeroed, ones_ready, ident_ready, half_ready = sem("zeroed"), sem("ones_ready"), sem("ident_ready"), sem("half_ready")
        x_turned, xT_hi, xT_ready = sem("x_turned"), sem("xT_hi"), sem("xT_ready")
        x_squared, x_rms_step, x_rms = sem("x_squared"), sem("x_rms_step"), sem("x_rms")
        xn_ready, xn_hi, xn_split = sem("xn_ready"), sem("xn_hi"), sem("xn_split")
        diag_ready, r_broadcast, r_row_ready = sem("diag_ready"), sem("r_broadcast"), sem("r_row_ready")
        h_added, h_squared, h_rms_step, h_rms = sem("h_added"), sem("h_squared"), sem("h_rms_step"), sem("h_rms")
        hg_ready, h_turned, hT_hi, hT_ready = sem("hg_ready"), sem("h_turned"), sem("hT_hi"), sem("hT_ready")
        qkv_copied, qk_squared, ssq_ready = sem("qkv_copied"), sem("qk_squared"), sem("ssq_ready")
        qk_rms_step, qk_rms = sem("qk_rms_step"), sem("qk_rms")
        qk_normed, qk_turned, qkT_ready = sem("qk_normed"), sem("qk_turned"), sem("qkT_ready")
        scores_ready, max_found, negmax_ready = sem("scores_ready"), sem("max_found"), sem("negmax_ready")
        exp_done, sums_inverted, probs_ready = sem("exp_done"), sem("sums_inverted"), sem("probs_ready")
        probs_turned, probsT_ready, o_ready = sem("probs_turned"), sem("probsT_ready"), sem("o_ready")
        o_hi, branch_split = sem("o_hi"), sem("branch_split")
        gate_copied, feat_taken = sem("gate_copied"), sem("feat_taken")
        gates_ready, conv_step = sem("gates_ready"), sem("conv_step")
        a_hi, m_sum, m_hi, m_ready = sem("a_hi"), sem("m_sum"), sem("m_hi"), sem("m_ready")
        wo_ready = sem("wo_ready")
        up_scaled, up_tap2, up_tap1, up_conv = sem("up_scaled"), sem("up_tap2"), sem("up_tap1"), sem("up_conv")
        silu_ready, s_product, s_hi, s_ready = sem("silu_ready"), sem("s_product"), sem("s_hi"), sem("s_ready")
        down_ready, out_ready = sem("down_ready"), sem("out_ready")

        def bank_pair(b):
            return b[:].rearrange("p (a t) -> p a t", a=2)

        def quarter(q):
            return slice(q % 4 * UNIT // 4, (q % 4 + 1) * UNIT // 4)

        def quarter_count(q):
            return q - q // 4 + 1

        block = ctx.enter_context(nc.Block())

        @block.sync
        def _(sp):
            def unit_at(n):
                return stream[bass.ds(n, 1), :, :].rearrange("a p n -> (a p) n")


            def load_x(c):
                cols = slice(c * D // 2, (c + 1) * D // 2)
                for t in range(TT):
                    sp.dma_start(x_tok[:, t, cols], x[t * P:(t + 1) * P, cols]).then_inc(x_landed[t][c], 16)

            def load_quarter(q):
                sp.dma_start(raw[:, q // 4, quarter(q)], stream[q // 4, :, quarter(q)]).then_inc(quarter_landed[q], 16)

            load_x(0)
            sp.dma_start(prm[:], params).then_inc(prm_landed, 16)
            load_quarter(0)
            load_quarter(1)
            load_x(1)
            for q in range(2, QUARTERS):
                load_quarter(q)
            sp.dma_start(raw[:, 3, :], stream[3, :, :]).then_inc(raw_landed[3], 16)
            with sp.Fori(1, U_FFN // SLOTS) as i:
                for s in range(SLOTS):
                    sp.wait_ge(lo_ready, i * SLOTS + (s + 1 - SLOTS))
                    sp.dma_start(raw[:, s, :], unit_at(i * SLOTS + s)).then_inc(raw_landed[s], 16)
            sp.wait_ge(feat_taken, U_OUTB - U_C)
            sp.dma_start(g_ffn, norm_ffn.to_broadcast([P, D])).then_inc(gffn_landed, 16)

            def load_ffn(slot, unit, split_before):
                sp.wait_ge(lo_ready, split_before)
                sp.dma_start(raw[:, slot, :], unit).then_inc(ffn_landed[slot], 16)

            for slot, pos, before in ((0, 0, -3), (1, 1, -2), (2, 2, -1), (3, 3, 0), (0, 4, 1),
                                      (1, 5, 2), (2, 6, 3), (3, 3 * PAIRS - 1, 4), (0, 7, 5)):
                load_ffn(slot, stream[U_FFN + pos, :, :], U_FFN + before)
            with sp.Fori(3, PAIRS) as j:
                for n, slot in enumerate((1, 2, 0)):
                    load_ffn(slot, unit_at(j * 3 + (U_FFN - 1 + n)), j * 3 + (U_FFN - 2 + n))
            for n, (t, c) in enumerate(OUT_PARTS):
                part = slice(c * HALF, (c + 1) * HALF)
                sp.wait_ge(out_ready, n + 1)
                sp.dma_start(out[t * P:(t + 1) * P, part], out_tok[:, t, part]).then_inc(out_stored, 16)
            sp.wait_ge(out_stored, 16 * len(OUT_PARTS))

        @block.gpsimd
        def _(pool):
            pool.memset(ones[:], 1.0).then_inc(ones_ready, 1)
            pool.memset(ident[:], 0.0).then_inc(zeroed, 1)
            pool.memset(ident_bf[:], 0.0).then_inc(zeroed, 1)
            pool.memset(mask_bf[:], 0.0).then_inc(zeroed, 1)
            pool.memset(half[:], -0.5).then_inc(half_ready, 1)
            pool.wait_ge(zeroed, 3)
            for m in (ident, ident_bf):
                pool.affine_select(out=m[:], in_=m[:], compare_op=ALU.not_equal, fill=1.0, base=0,
                                   pattern=[[-1, P]], channel_multiplier=1).then_inc(ident_ready, 1)
            pool.affine_select(out=mask_bf[:], in_=mask_bf[:], compare_op=ALU.is_ge, fill=MASKED, base=0,
                               pattern=[[-1, P]], channel_multiplier=1).then_inc(ident_ready, 1)
            pool.wait_ge(half_ready, 1)
            for t in range(TT):
                pool.wait_ge(x_squared, t + 1)
                pool.tensor_scalar(sst[:, t:t + 1], ssx[:, t:t + 1], 1.0 / D, EPS, ALU.mult, ALU.add).then_inc(x_rms_step, 1)
                pool.wait_ge(x_rms_step, t + 1)
                pool.tensor_tensor(rx[:, t:t + 1], sst[:, t:t + 1], half[:, 0:1], ALU.pow).then_inc(x_rms, 1)
            pool.wait_ge(ssq_ready, 4)
            pool.tensor_scalar(rqk[:], ssq[:], 1.0 / P, EPS, ALU.mult, ALU.add).then_inc(qk_rms_step, 1)
            pool.wait_ge(qk_rms_step, 1)
            pool.tensor_tensor(rqk[:].rearrange("p t s h -> p (t s h)"), rqk[:].rearrange("p t s h -> p (t s h)"),
                               half[:], ALU.pow).then_inc(qk_rms, 1)
            for t in range(TT):
                pool.wait_ge(h_squared, TT + t + 1)
                pool.tensor_tensor(rh[:, t:t + 1], ssh[:, t, 0:1], ssh[:, t, 1:2], ALU.add).then_inc(h_rms_step, 1)
                pool.wait_ge(h_rms_step, 2 * t + 1)
                pool.tensor_scalar(sst[:, t:t + 1], rh[:, t:t + 1], 1.0 / D, EPS, ALU.mult, ALU.add).then_inc(h_rms_step, 1)
                pool.wait_ge(h_rms_step, 2 * t + 2)
                pool.tensor_tensor(rh[:, t:t + 1], sst[:, t:t + 1], half[:, 0:1], ALU.pow).then_inc(h_rms, 1)

        @block.scalar
        def _(act):
            def split_hi(slot, landed, count, used=None):
                act.wait_ge(landed[slot], count)
                if used is not None:
                    act.wait_ge(weights_used, used)
                act.activation(w_hi[:, slot, :], raw[:, slot, :], ACT.Copy).then_inc(hi_ready, 1)

            def split_ahead(slot, i):
                split_hi(slot, raw_landed, i * 16 + 16, i * SLOTS + (slot + 1 - SLOTS))

            def split_step(n):
                split_ahead(n % SLOTS, n // SLOTS + 1)

            def quarter_hi_part(q):
                act.wait_ge(quarter_landed[q], 16)
                act.activation(w_hi[:, q // 4, quarter(q)], raw[:, q // 4, quarter(q)],
                               ACT.Copy).then_inc(hi_ready if q % 4 == 3 else quarter_hi, 1)

            act.wait_ge(half_ready, 1)
            act.activation(mx[:, 0, :], half[:, 0:2], ACT.Copy)
            act.wait_ge(prm_landed, 16)
            quarter_hi_part(0)
            for b in range(4):
                act.wait_ge(x_turned, b + 1)
                for k in (2 * b, 2 * b + 1):
                    ins = act.activation(acts[:, 1, 0, k, :], tb[b][:, (k % 2) * SEQ:(k % 2 + 1) * SEQ], ACT.Copy,
                                         scale=prm[:, PC_NM + k:PC_NM + k + 1])
                ins.then_inc(xT_hi, 1)
                quarter_hi_part(2 * b + 1)
                if b < 3:
                    quarter_hi_part(2 * b + 2)
            for t in range(TT):
                for c in range(2):
                    act.wait_ge(x_landed[t][c], 16)
                if t:
                    act.wait_ge(x_squared, t)
                act.activation(junk_x, x_tok[:, t, :], ACT.Square, accum_out=ssx[:, t:t + 1]).then_inc(x_squared, 1)
            for q in range(KT, QUARTERS):
                quarter_hi_part(q)
            split_hi(3, raw_landed, 16)

            def qkv_section(i, squares):
                for s in range(SLOTS):
                    if not squares and s == 0:
                        act.wait_ge(xn_ready, 1)
                        act.activation(acts[:, 2, 0, :, :], xn_feat, ACT.Copy).then_inc(xn_hi, 1)
                    if not squares and s == 3:
                        take_qkT(0)
                    if s % 2:
                        c = s // 2
                        act.wait_ge(weights_used, i * SLOTS + (s + 1))
                        if not squares and c == 0:
                            act.wait_ge(xn_split, 1)
                        for t in range(TT):
                            done = act.activation(qkv[:, bass.ds(i, 1), t, c * 512:(c + 1) * 512].rearrange("p a d -> p (a d)"),
                                                  zb[2 * c + t][:], ACT.Copy, scale=rx[:, t:t + 1])
                            if not squares:
                                done.then_inc(qkv_copied, 1)
                        if squares:
                            for t in range(TT):
                                act.activation(sq_tmp[:, t, :], zb[2 * c + t][:], ACT.Square,
                                               scale=rx[:, t:t + 1]).then_inc(qk_squared, 1)
                    split_ahead(s, i + 1)
                    if s % 2 and squares:
                        act.wait_ge(ssq_ready, i * 2 + (c + 1))

            def take_qkT(u):
                act.wait_ge(qk_turned, u + 1)
                if u >= 2:
                    act.wait_ge(scores_ready, u - 1)
                act.activation(qkT[:, u % 2, 0, :], qkT_ps[:, 0:SEQ], ACT.Copy, scale=prm[:, PC_QN:PC_QN + 1])
                act.activation(qkT[:, u % 2, 1, :], qkT_ps[:, SEQ:2 * SEQ], ACT.Copy,
                               scale=prm[:, PC_KN:PC_KN + 1]).then_inc(qkT_ready, 1)

            act.wait_ge(x_rms, TT)
            with act.Fori(0, SEC_V) as i:
                qkv_section(i, True)
            qkv_section(SEC_V, False)

            for u in range(HEADS):
                par = u % 2
                n = U_GA + u
                if u:
                    split_step(n - 1)
                act.wait_ge(negmax_ready, u + 1)
                if u >= 2:
                    act.wait_ge(probs_turned, u - 1)
                act.activation(probs[:, par, 0:2, :], score_ps[:, 0:SEQ].rearrange("p (a k) -> p a k", a=2), ACT.Exp,
                               bias=negmx[:, par, 0:1], scale=SCALE, accum_out=psums[:, par, 0:1])
                act.activation(probs[:, par, 2, :], score_ps[:, SEQ:SEQ + P], ACT.Exp,
                               bias=negmx[:, par, 1:2], scale=SCALE, accum_out=psums[:, par, 1:2]).then_inc(exp_done, 1)
                if u + 1 < HEADS:
                    take_qkT(u + 1)
                act.wait_ge(weights_used, n + 1)
                act.activation(gates[:, u // 4, 2 * (u % 4):2 * (u % 4) + 2, :], bank_pair(zb[n % 4]),
                               ACT.Copy).then_inc(gate_copied, 1)

            for n in range(U_C, U_B):
                split_step(n - 1)
                if n % 4 == 1:
                    g = (n - U_C) // 4
                    act.wait_ge(gate_copied, 4 * (g + 1))
                    act.activation(gates[:, g, :, :], gates[:, g, :, :], ACT.Sigmoid).then_inc(gates_ready, 1)
            for u in range(4):
                n = U_B + u
                split_step(n - 1)
                act.wait_ge(feat_taken, n + 1 - U_C)
                act.activation(acts[:, 1, 0, 2 * u:2 * u + 2, :], a_feat[:, 2 * u:2 * u + 2, :], ACT.Copy).then_inc(a_hi, 1)
            for n in range(U_OUTB, U_OUTA):
                split_step(n - 1)
            split_step(U_OUTA - 1)
            for u in range(4):
                split_step(U_OUTA + u)
                act.wait_ge(m_sum, u + 1)
                act.activation(acts[:, 2, 0, 2 * u:2 * u + 2, :], br_feat[:, 2 * u:2 * u + 2, :], ACT.Copy).then_inc(m_hi, 1)

            def h_squares(b):
                c, t = divmod(b, 2)
                act.wait_ge(h_added, b + 1)
                act.activation(junk_h[:, t, c, :], x_tok[:, t, c * 512:(c + 1) * 512], ACT.Square,
                               accum_out=ssh[:, t, c:c + 1]).then_inc(h_squared, 1)

            def hT_hi_part(b):
                c, t = divmod(b, 2)
                act.wait_ge(h_turned, b + 1)
                act.activation(acts[:, 1, 0, 4 * c:4 * c + 4, t * P:(t + 1) * P], tb[b][:].rearrange("p (k t) -> p k t", k=4),
                               ACT.Copy).then_inc(hT_hi, 1)

            h_squares(0)
            h_squares(1)
            hT_hi_part(0)
            split_hi(0, ffn_landed, 16, U_FFN - 2)
            split_hi(1, ffn_landed, 16, U_FFN - 2)
            h_squares(2)
            hT_hi_part(1)
            hT_hi_part(2)
            hT_hi_part(3)
            h_squares(3)
            split_hi(2, ffn_landed, 16, U_FFN)
            split_hi(3, ffn_landed, 16, U_FFN)

            def tap2(u, j):
                for g in range(2):
                    act.wait_ge(up_scaled, j * 4 + (2 * u + g + 1))
                    if g == 0 and not (isinstance(j, int) and j == 0):
                        act.wait_ge(s_product, j * 2 + (u - 1))
                    col = j * 4 + (2 * u + g)
                    act.activation(y_up[:, u, g, :], up_sc[:, u, g, :], ACT.Identity,
                                   scale=prm[:, bass.ds(col * 3 + (PC_FW + 2), 1)],
                                   bias=prm[:, bass.ds(col + PC_FB, 1)]).then_inc(up_tap2, 1)

            def silu(u, halves):
                act.wait_ge(up_conv, halves)
                act.activation(silu_g[:, u, :], y_up[:, u, 0, :], ACT.Silu).then_inc(silu_ready, 1)

            def hidden_hi(tiles, used, region=0):
                act.wait_ge(s_product, tiles)
                if used is not None:
                    act.wait_ge(weights_used, used)
                act.activation(acts[:, region, 0, 0:2, :], s_pair, ACT.Copy).then_inc(s_hi, 1)

            split_hi(0, ffn_landed, 32, U_FFN + 1)
            tap2(0, 0)
            split_hi(1, ffn_landed, 32, U_FFN + 2)
            silu(0, 1)
            tap2(1, 0)
            split_hi(2, ffn_landed, 32, U_FFN + 3)
            silu(1, 3)
            hidden_hi(2, None)
            tap2(0, 1)
            silu(0, 5)
            tap2(1, 1)
            split_hi(3, ffn_landed, 32, U_FFN + 4)
            with act.Fori(2, PAIRS - 1) as j:
                split_hi(0, ffn_landed, j * 16 + 16, j * 3 + (U_FFN - 1))
                silu(1, j * 4 - 1)
                hidden_hi(j * 2, j * 3 + (U_FFN - 1))
                split_hi(1, ffn_landed, j * 16 + 16, j * 3 + U_FFN)
                tap2(0, j)
                split_hi(2, ffn_landed, j * 16 + 16, j * 3 + (U_FFN + 1))
                silu(0, j * 4 + 1)
                tap2(1, j)
            j = PAIRS - 1
            split_hi(0, ffn_landed, j * 16 + 16, j * 3 + (U_FFN - 1))
            silu(1, j * 4 - 1)
            hidden_hi(j * 2, j * 3 + (U_FFN - 1))
            for u in range(2):
                tap2(u, j)
                silu(u, j * 4 + 2 * u + 1)
                act.wait_ge(s_product, j * 2 + u + 1)
                act.activation(acts[:, 2, 0, u, :], s_pair[:, u, :], ACT.Copy).then_inc(s_hi, 1)

        @block.vector
        def _(dve):
            def split_lo(slot, count):
                dve.wait_ge(hi_ready, count)
                dve.tensor_tensor(w_lo[:, slot, :], raw[:, slot, :], w_hi[:, slot, :].bitcast(F32),
                                  ALU.subtract).then_inc(lo_ready, 1)

            def quarter_lo_part(q):
                if q % 4 == 3:
                    dve.wait_ge(hi_ready, q // 4 + 1)
                else:
                    dve.wait_ge(quarter_hi, quarter_count(q))
                dve.tensor_tensor(w_lo[:, q // 4, quarter(q)], raw[:, q // 4, quarter(q)],
                                  w_hi[:, q // 4, quarter(q)].bitcast(F32), ALU.subtract).then_inc(
                                      lo_ready if q % 4 == 3 else quarter_lo, 1)

            def broadcast_rms(r, rms):
                dve.wait_ge(rms, TT)
                for t in range(TT):
                    ins = dve.tensor_scalar(diag[:, t, :], ident[:], r[:, t:t + 1], None, ALU.mult)
                ins.then_inc(diag_ready, 1)

            def take_r_row(which, count):
                dve.wait_ge(r_broadcast, count)
                dve.tensor_copy(r_row[:], r_ps[which][:, 0:SEQ]).then_inc(r_row_ready, 1)
                dve.wait_ge(r_row_ready, count)

            dve.wait_ge(prm_landed, 16)
            dve.wait_ge(ident_ready, 3)
            quarter_lo_part(0)
            for b in range(4):
                dve.wait_ge(xT_hi, b + 1)
                for k in (2 * b, 2 * b + 1):
                    dve.scalar_tensor_tensor(out=acts[:, 1, 1, k, :], in0=tb[b][:, (k % 2) * SEQ:(k % 2 + 1) * SEQ],
                                             scalar=prm[:, PC_NM + k:PC_NM + k + 1], in1=acts[:, 1, 0, k, :].bitcast(F32),
                                             op0=ALU.mult, op1=ALU.subtract).then_inc(xT_ready, 1)
                quarter_lo_part(2 * b + 1)
                if b < 3:
                    quarter_lo_part(2 * b + 2)
            broadcast_rms(rx, x_rms)
            for q in range(KT, QUARTERS):
                quarter_lo_part(q)
            take_r_row("x", 1)
            split_lo(3, 4)
            for k in range(KT):
                ins = dve.scalar_tensor_tensor(out=xn_feat[:, k, :], in0=tb[k // 2][:, (k % 2) * SEQ:(k % 2 + 1) * SEQ],
                                               scalar=prm[:, PC_NM + k:PC_NM + k + 1], in1=r_row[:], op0=ALU.mult, op1=ALU.mult)
            ins.then_inc(xn_ready, 1)

            def qkv_section(i, squares):
                for s in range(SLOTS):
                    if squares and s % 2:
                        c = s // 2
                        dve.wait_ge(qk_squared, i * 4 + (2 * c + 2))
                        dve.tensor_reduce(ssq[:, :, bass.ds(i, 1), 4 * c:4 * c + 4].rearrange("p t s h -> p t (s h)"),
                                          sq_tmp[:].rearrange("p t (h d) -> p t h d", h=4),
                                          axis=AX_X, op=ALU.add).then_inc(ssq_ready, 1)
                    if not squares and s == 0:
                        dve.wait_ge(xn_hi, 1)
                        dve.tensor_tensor(acts[:, 2, 1, :, :], xn_feat, acts[:, 2, 0, :, :].bitcast(F32),
                                          ALU.subtract).then_inc(xn_split, 1)
                    if not squares and s in (1, 2):
                        norm_qk(s - 1)
                    split_lo(s, i * SLOTS + (s + 5))

            def norm_qk(h):
                dve.wait_ge(qk_rms, 1)
                for t in range(TT):
                    view = qkv[:, 0:2, t, h * P:(h + 1) * P]
                    ins = dve.tensor_tensor(view, view, rqk[:, t, :, h:h + 1].to_broadcast([P, 2, P]), ALU.mult)
                ins.then_inc(qk_normed, 1)

            with dve.Fori(0, SEC_V) as i:
                qkv_section(i, True)
            qkv_section(SEC_V, False)

            def attention_tail(h):
                par = h % 2
                dve.wait_ge(probs_turned, h + 1)
                if h >= 2:
                    dve.wait_ge(o_ready, h - 1)
                dve.tensor_copy(probsT[:, par, :, :], probsT_ps[:, 0:3 * P].rearrange("p (a q) -> p a q", a=3)).then_inc(probsT_ready, 1)

            def attention_out(h):
                dve.wait_ge(o_ready, h + 1)
                dve.tensor_copy(acts[:, 0, 0, h, :], o_ps[:, 0:SEQ]).then_inc(o_hi, 1)
                dve.wait_ge(o_hi, h + 1)
                dve.tensor_tensor(acts[:, 0, 1, h, :], o_ps[:, 0:SEQ], acts[:, 0, 0, h, :].bitcast(F32),
                                  ALU.subtract).then_inc(branch_split, 1)

            for u in range(HEADS):
                par = u % 2
                n = U_GA + u
                if u + 2 < HEADS:
                    norm_qk(u + 2)
                dve.wait_ge(scores_ready, u + 1)
                dve.reduce_max(mx[:, par, 0:1], score_ps[:, 0:SEQ], AX_X)
                dve.reduce_max(mx[:, par, 1:2], score_ps[:, SEQ:SEQ + P], AX_X).then_inc(max_found, 1)
                dve.wait_ge(max_found, u + 1)
                dve.tensor_scalar(negmx[:, par, :], mx[:, par, :], -SCALE, None, ALU.mult).then_inc(negmax_ready, 1)
                if u:
                    attention_tail(u - 1)
                    split_lo((n + 3) % SLOTS, n + 4)
                dve.wait_ge(exp_done, u + 1)
                dve.reciprocal(rsums[:, par, :], psums[:, par, :]).then_inc(sums_inverted, 1)
                dve.wait_ge(sums_inverted, u + 1)
                dve.tensor_scalar(probs[:, par, 0:2, :], probs[:, par, 0:2, :], rsums[:, par, 0:1], None, ALU.mult)
                dve.tensor_scalar(probs[:, par, 2, :], probs[:, par, 2, :], rsums[:, par, 1:2], None,
                                  ALU.mult).then_inc(probs_ready, 1)
                if u:
                    attention_out(u - 1)

            for u in range(4):
                n = U_C + u
                split_lo((n + 3) % SLOTS, n + 4)
                if u == 0:
                    attention_tail(HEADS - 1)
                dve.wait_ge(weights_used, n + 1)
                dve.tensor_copy(u_feat[:, 2 * u:2 * u + 2, :], bank_pair(zb[n % 4])).then_inc(feat_taken, 1)
                if u == 0:
                    attention_out(HEADS - 1)
            dve.wait_ge(prm_landed, 16)
            for u in range(4):
                n = U_X + u
                split_lo((n + 3) % SLOTS, n + 4)
                two = slice(2 * u, 2 * u + 2)
                dve.wait_ge(weights_used, n + 1)
                if u == 0:
                    dve.wait_ge(feat_taken, 4)
                dve.tensor_tensor(u_feat[:, two, :], bank_pair(zb[n % 4]), u_feat[:, two, :], ALU.mult).then_inc(feat_taken, 1)
                dve.wait_ge(feat_taken, 5 + u)
                for tap in (2, 1, 0):
                    shift = 2 - tap
                    for k in (2 * u, 2 * u + 1):
                        w = prm[:, PC_CONV_A + 3 * k + tap:PC_CONV_A + 3 * k + tap + 1]
                        if tap == 2:
                            ins = dve.tensor_scalar(conv_feat[:, k, :], u_feat[:, k, :], w, None, ALU.mult)
                        else:
                            ins = dve.scalar_tensor_tensor(out=conv_feat[:, k, shift:SEQ], in0=u_feat[:, k, 0:SEQ - shift],
                                                           scalar=w, in1=conv_feat[:, k, shift:SEQ], op0=ALU.mult, op1=ALU.add)
                    ins.then_inc(conv_step, 1)
                    dve.wait_ge(conv_step, 3 * u + 3 - tap)
            def a_lo(u):
                two = slice(2 * u, 2 * u + 2)
                dve.wait_ge(a_hi, u + 1)
                ins = dve.tensor_tensor(acts[:, 1, 1, two, :], a_feat[:, two, :], acts[:, 1, 0, two, :].bitcast(F32), ALU.subtract)
                ins.then_inc(branch_split, 1)

            for u in range(4):
                n = U_B + u
                two = slice(2 * u, 2 * u + 2)
                split_lo((n + 3) % SLOTS, n + 4)
                dve.wait_ge(weights_used, n + 1)
                dve.tensor_tensor(a_feat[:, two, :], bank_pair(zb[n % 4]), conv_feat[:, two, :], ALU.mult).then_inc(feat_taken, 1)
                a_lo(u)
            for u in range(4):
                n = U_OUTB + u
                two = slice(2 * u, 2 * u + 2)
                split_lo((n + 3) % SLOTS, n + 4)
                dve.wait_ge(weights_used, n + 1)
                if u == 0:
                    dve.wait_ge(gates_ready, 2)
                dve.tensor_tensor(br_feat[:, two, :], bank_pair(zb[n % 4]), gates[:, 1, two, :], ALU.mult).then_inc(feat_taken, 1)
            split_lo((U_OUTA + 3) % SLOTS, U_OUTA + 4)
            for u in range(4):
                n = U_OUTA + u
                two = slice(2 * u, 2 * u + 2)
                dve.wait_ge(weights_used, n + 1)
                dve.tensor_tensor(u_feat[:, two, :], bank_pair(zb[n % 4]), gates[:, 0, two, :], ALU.mult).then_inc(feat_taken, 1)
                dve.wait_ge(feat_taken, n + 1 - U_C)
                dve.tensor_tensor(br_feat[:, two, :], u_feat[:, two, :], br_feat[:, two, :], ALU.add).then_inc(m_sum, 1)
                if u < 3:
                    split_lo(n % SLOTS, n + 5)
                dve.wait_ge(m_hi, u + 1)
                dve.tensor_tensor(acts[:, 2, 1, two, :], br_feat[:, two, :], acts[:, 2, 0, two, :].bitcast(F32),
                                  ALU.subtract).then_inc(m_ready, 1)
            split_lo(3, U_WO + 4)

            def add_h(b):
                c, t = divmod(b, 2)
                if t == 0:
                    dve.wait_ge(wo_ready, c + 1)
                else:
                    dve.wait_ge(weights_used, U_WO + 2 * (c + 1))
                part = x_tok[:, t, c * 512:(c + 1) * 512]
                dve.tensor_tensor(part, zb[b][:], part, ALU.add).then_inc(h_added, 1)
                dve.wait_ge(h_added, b + 1)
                dve.tensor_tensor(hg_tok[:, t, c * 512:(c + 1) * 512], part, g_ffn[:, c * 512:(c + 1) * 512],
                                  ALU.mult).then_inc(hg_ready, 1)

            def hT_lo_part(b):
                c, t = divmod(b, 2)
                dve.wait_ge(hT_hi, b + 1)
                dve.tensor_tensor(acts[:, 1, 1, 4 * c:4 * c + 4, t * P:(t + 1) * P], tb[b][:].rearrange("p (k t) -> p k t", k=4),
                                  acts[:, 1, 0, 4 * c:4 * c + 4, t * P:(t + 1) * P].bitcast(F32), ALU.subtract).then_inc(hT_ready, 1)

            dve.wait_ge(gffn_landed, 16)
            add_h(0)
            add_h(1)
            hT_lo_part(0)
            split_lo(0, U_FFN + 1)
            add_h(2)
            split_lo(1, U_FFN + 2)
            hT_lo_part(1)
            hT_lo_part(2)
            add_h(3)
            hT_lo_part(3)
            broadcast_rms(rh, h_rms)
            split_lo(2, U_FFN + 3)
            take_r_row("h", 2)
            split_lo(3, U_FFN + 4)

            def scale_up(u, j):
                first = isinstance(j, int) and j == 0
                dve.wait_ge(weights_used, U_FFN + 1 + u if first else j * 3 + (U_FFN + u))
                for g in range(2):
                    dve.tensor_tensor(up_sc[:, u, g, :], upb[u][:, g * SEQ:(g + 1) * SEQ], r_row[:],
                                      ALU.mult).then_inc(up_scaled, 1)

            def taps(u, j):
                for tap, before, signal in ((1, up_tap2, up_tap1), (0, up_tap1, up_conv)):
                    shift = 2 - tap
                    for g in range(2):
                        dve.wait_ge(before, j * 4 + (2 * u + g + 1))
                        y = y_up[:, u, g, shift:SEQ]
                        w = prm[:, bass.ds((j * 4 + (2 * u + g)) * 3 + (PC_FW + tap), 1)]
                        dve.scalar_tensor_tensor(out=y, in0=up_sc[:, u, g, 0:SEQ - shift], scalar=w, in1=y,
                                                 op0=ALU.mult, op1=ALU.add).then_inc(signal, 1)

            def hidden(u, done):
                dve.wait_ge(silu_ready, done)
                dve.wait_ge(up_conv, done * 2)
                dve.tensor_tensor(s_pair[:, u, :], silu_g[:, u, :], y_up[:, u, 1, :], ALU.mult).then_inc(s_product, 1)

            def hidden_lo(pairs):
                dve.wait_ge(s_hi, pairs)
                dve.tensor_tensor(acts[:, 0, 1, 0:2, :], s_pair, acts[:, 0, 0, 0:2, :].bitcast(F32),
                                  ALU.subtract).then_inc(s_ready, 1)

            scale_up(0, 0)
            split_lo(0, U_FFN + 5)
            taps(0, 0)
            scale_up(1, 0)
            split_lo(1, U_FFN + 6)
            hidden(0, 1)
            taps(1, 0)
            hidden(1, 2)
            scale_up(0, 1)
            hidden_lo(1)
            split_lo(2, U_FFN + 7)
            taps(0, 1)
            scale_up(1, 1)
            hidden(0, 3)
            taps(1, 1)
            split_lo(3, U_FFN + 8)
            with dve.Fori(2, PAIRS - 1) as j:
                split_lo(0, j * 3 + (U_FFN + 3))
                hidden(1, j * 2)
                hidden_lo(j)
                scale_up(0, j)
                split_lo(1, j * 3 + (U_FFN + 4))
                taps(0, j)
                scale_up(1, j)
                split_lo(2, j * 3 + (U_FFN + 5))
                hidden(0, j * 2 + 1)
                taps(1, j)
            j = PAIRS - 1
            split_lo(0, j * 3 + (U_FFN + 3))
            hidden(1, j * 2)
            hidden_lo(j)
            for u in range(2):
                scale_up(u, j)
                taps(u, j)
                hidden(u, j * 2 + u + 1)
                dve.wait_ge(s_hi, PAIRS + u)
                dve.tensor_tensor(acts[:, 2, 1, u, :], s_pair[:, u, :], acts[:, 2, 0, u, :].bitcast(F32),
                                  ALU.subtract).then_inc(s_ready, 1)
            for n, (t, c) in enumerate(OUT_PARTS):
                part = slice(c * HALF, (c + 1) * HALF)
                dve.wait_ge(down_ready, n + 1)
                dve.tensor_tensor(out_tok[:, t, part], zb[2 * t + c][:], x_tok[:, t, part], ALU.add).then_inc(out_ready, 1)

        @block.tensor
        def _(pe):
            def three_pass(out_, st, mv, start, stop):
                pe.matmul(out_, st(0), mv(0), start=start, stop=False)
                pe.matmul(out_, st(0), mv(1), start=False, stop=False)
                return pe.matmul(out_, st(1), mv(0), start=False, stop=stop)

            def weights(part, slot):
                return (w_hi, w_lo)[part][:, slot, :]

            def feature_tile(slot, a, bank, region, half=None):
                for k in range(KT) if half is None else range(4 * half, 4 * half + 4):
                    last = three_pass(
                        bank[:, a * SEQ:(a + 1) * SEQ],
                        lambda h: weights(h, slot)[:, k * 256 + a * P:k * 256 + (a + 1) * P],
                        lambda h: acts[:, region, h, k, :] if isinstance(region, int) else
                        acts[:, bass.ds(region, 1), h, k, :].rearrange("p a t -> p (a t)"),
                        k == 0, k == KT - 1)
                return last

            def token_product(slot, k, t, bank, region):
                return three_pass(bank[:], lambda h: acts[:, region, h, k, t * P:(t + 1) * P],
                                  lambda h: weights(h, slot)[:, (k % 4) * 512:(k % 4 + 1) * 512], k == 0, k == KT - 1)

            def broadcast(which, count):
                pe.wait_ge(diag_ready, count)
                for t in range(TT):
                    ins = pe.matmul(r_ps[which][:, t * P:(t + 1) * P], ones[:], diag[:, t, :], start=True, stop=True)
                ins.then_inc(r_broadcast, 1)

            def turn_x(c):
                for t in range(TT):
                    pe.wait_ge(x_landed[t][c], 16)
                    for k in range(4 * c, 4 * c + 4):
                        ins = pe.transpose(tb[k // 2][:, (k % 2) * SEQ + t * P:(k % 2) * SEQ + (t + 1) * P],
                                           x_tok[:, t, k * P:(k + 1) * P], ident[:])
                        if t == TT - 1 and k % 2:
                            ins.then_inc(x_turned, 1)

            def keep_busy(n):
                for _ in range(n):
                    pe.matmul(banks[0][:, 0:P], ones[:], ones[:], start=True, stop=True)

            pe.wait_ge(ones_ready, 1)
            keep_busy(WARM_UPS[0])
            pe.wait_ge(ident_ready, 3)
            turn_x(0)
            keep_busy(WARM_UPS[1])

            def qkv_section(i, first):
                for c in range(2):
                    if not first:
                        pe.wait_ge(qk_squared, i * 4 + (2 * c - 2))
                    for kh in range(2):
                        slot = 2 * c + kh
                        if not first or slot == 3:
                            pe.wait_ge(lo_ready, i * SLOTS + (slot + 1))
                        for k in range(4 * kh, 4 * kh + 4):
                            q = 4 * slot + k % 4
                            if first and q < QUARTERS:
                                if q % 4 == 3:
                                    pe.wait_ge(lo_ready, slot + 1)
                                else:
                                    pe.wait_ge(quarter_lo, quarter_count(q))
                            if first and c == 0:
                                pe.wait_ge(xT_ready, k + 1)
                            for t in range(TT):
                                if first and c and k == 0 and t == TT - 1:
                                    pe.wait_ge(r_row_ready, 1)
                                last = token_product(slot, k, t, zb[2 * c + t], 1)
                            if first and q == 0:
                                turn_x(1)
                        last.then_inc(weights_used, 1)
                        if first and slot == 1:
                            broadcast("x", 1)

            qkv_section(0, True)
            with pe.Fori(1, SEC_V + 1) as i:
                qkv_section(i, False)
            pe.wait_ge(xn_split, 1)

            def turn_qk(h):
                pe.wait_ge(qk_normed, h + 1)
                if h:
                    pe.wait_ge(qkT_ready, h)
                for s in range(2):
                    for t in range(TT):
                        last = pe.transpose(qkT_ps[:, s * SEQ + t * P:s * SEQ + (t + 1) * P],
                                            qkv[:, s, t, h * P:(h + 1) * P], ident[:])
                last.then_inc(qk_turned, 1)

            def scores(h):
                pe.wait_ge(qkT_ready, h + 1)
                if h:
                    pe.wait_ge(exp_done, h)
                q, k = qkT[:, h % 2, 0, :], qkT[:, h % 2, 1, :]
                pe.matmul(score_ps[:, 0:SEQ], q[:, P:SEQ], k, start=True, stop=False)
                pe.matmul(score_ps[:, P:SEQ], ident_bf[:], mask_bf[:], start=False, stop=True)
                pe.matmul(score_ps[:, SEQ:SEQ + P], q[:, 0:P], k[:, 0:P], start=True, stop=False)
                pe.matmul(score_ps[:, SEQ:SEQ + P], ident_bf[:], mask_bf[:], start=False, stop=True).then_inc(scores_ready, 1)

            def turn_probs(h):
                pe.wait_ge(probs_ready, h + 1)
                if h:
                    pe.wait_ge(probsT_ready, h)
                for src, dst in ((2, 0), (0, 1), (1, 2)):
                    last = pe.transpose(probsT_ps[:, dst * P:(dst + 1) * P], probs[:, h % 2, src, :], ident[:])
                last.then_inc(probs_turned, 1)

            def weigh_values(h):
                pe.wait_ge(probsT_ready, h + 1)
                if h:
                    pe.wait_ge(branch_split, h)
                pT = probsT[:, h % 2, :, :].rearrange("p a q -> p (a q)")
                pe.matmul(o_ps[:, 0:SEQ], qkv[:, 2, 0, h * P:(h + 1) * P], pT[:, 0:SEQ], start=True, stop=False)
                pe.matmul(o_ps[:, P:SEQ], qkv[:, 2, 1, h * P:(h + 1) * P], pT[:, SEQ:SEQ + P], start=False,
                          stop=True).then_inc(o_ready, 1)

            for u in range(U_X - U_GA):
                n = U_GA + u
                slot = n % SLOTS
                if u < HEADS:
                    turn_qk(u)
                pe.wait_ge(lo_ready, n + 1)
                if u < 4:
                    pe.wait_ge(qkv_copied, 2 * (u // 2) + 2)
                else:
                    pe.wait_ge(gate_copied, u - 3)
                feature_tile(slot, 0, zb[slot], 2)
                if u < HEADS:
                    scores(u)
                if 0 < u <= HEADS:
                    turn_probs(u - 1)
                feature_tile(slot, 1, zb[slot], 2).then_inc(weights_used, 1)
                if 0 < u <= HEADS:
                    weigh_values(u - 1)

            def feature_section(i, first_unit, region):
                for s in range(SLOTS):
                    pe.wait_ge(lo_ready, i * SLOTS + (first_unit + s + 1))
                    pe.wait_ge(feat_taken, i * SLOTS + (first_unit + s + 1 - U_X))
                    feature_tile(s, 0, zb[s], region)
                    feature_tile(s, 1, zb[s], region).then_inc(weights_used, 1)

            with pe.Fori(0, 2) as i:
                feature_section(i, U_X, 2)
            with pe.Fori(0, 2) as i:
                pe.wait_ge(branch_split, i * 4 + HEADS)
                feature_section(i, U_OUTB, i)

            def turn_h(b):
                c, t = divmod(b, 2)
                pe.wait_ge(hg_ready, b + 1)
                for k in range(4):
                    ins = pe.transpose(tb[b][:, k * P:(k + 1) * P], hg_tok[:, t, (4 * c + k) * P:(4 * c + k + 1) * P], ident[:])
                ins.then_inc(h_turned, 1)

            def wo_half(b, kh):
                c, t = divmod(b, 2)
                if t == 0:
                    pe.wait_ge(lo_ready, U_WO + 2 * c + kh + 1)
                for k in range(4 * kh, 4 * kh + 4):
                    if b == 0 and k % 2 == 0:
                        pe.wait_ge(m_ready, k // 2 + 1)
                    last = token_product(2 * c + kh, k, t, zb[b], 2)
                if kh:
                    last.then_inc(wo_ready, 1) if t == 0 else last.then_inc(weights_used, 2)

            for b in range(2 * TT):
                wo_half(b, 0)
                if b == 3:
                    turn_h(2)
                wo_half(b, 1)
                if b in (1, 2):
                    turn_h(b - 1)
            for u in range(2):
                pe.wait_ge(hT_ready, 2)
                pe.wait_ge(lo_ready, U_FFN + 1 + u)
                feature_tile(u, 0, upb[u], 1, half=0)
                if u == 0:
                    turn_h(3)
            pe.wait_ge(hT_ready, 4)
            for u in range(2):
                feature_tile(u, 0, upb[u], 1, half=1)
                feature_tile(u, 1, upb[u], 1).then_inc(weights_used, 1)
                if u == 0:
                    broadcast("h", 2)

            def up(u, slot, split, scaled):
                pe.wait_ge(lo_ready, split)
                pe.wait_ge(up_scaled, scaled)
                feature_tile(slot, 0, upb[u], 1)
                feature_tile(slot, 1, upb[u], 1).then_inc(weights_used, 1)

            def down_part(slot, kk, t, c, region, start, stop):
                return three_pass(zb[2 * t + c][:], lambda h: acts[:, region, h, kk, t * P:(t + 1) * P],
                                  lambda h: weights(h, slot)[:, kk * D + c * HALF:kk * D + (c + 1) * HALF], start, stop)

            def down(split, pairs, start=False):
                pe.wait_ge(lo_ready, split)
                pe.wait_ge(s_ready, pairs)
                for t, c in OUT_PARTS:
                    for kk in range(2):
                        last = down_part(0, kk, t, c, 0, start and kk == 0, False)
                last.then_inc(weights_used, 1)

            up(0, 2, U_FFN + 3, 2)
            up(1, 3, U_FFN + 4, 4)
            pe.wait_ge(h_added, 4)
            down(U_FFN + 5, 1, start=True)
            with pe.Fori(2, PAIRS) as j:
                up(0, 1, j * 3 + (U_FFN + 1), j * 4 - 2)
                up(1, 2, j * 3 + (U_FFN + 2), j * 4)
                down(j * 3 + (U_FFN + 3), j)
            for kk in range(2):
                pe.wait_ge(s_ready, PAIRS + kk)
                for t, c in OUT_PARTS:
                    last = down_part(3, kk, t, c, 2, False, kk == 1)
                    if kk:
                        last.then_inc(down_ready, 1)


def weight_stream(w_in, w_out_a, w_out_b, w_o, w_up, w_down):
    import numpy as np

    def token(w):
        return w.reshape(2, 4, P, 2, 512).transpose(3, 0, 2, 1, 4).reshape(4, P, UNIT)

    def feature(w):
        return w.reshape(KT, P, 4, 256).transpose(2, 1, 0, 3).reshape(4, P, UNIT)

    b, c, x, q, k, v, ga, gb = (w_in[:, i * D:(i + 1) * D] for i in range(8))
    up = w_up.reshape(KT, P, 2, FT, P).transpose(3, 1, 0, 2, 4).reshape(FT, P, UNIT)
    down = w_down.reshape(PAIRS, 2, P, D).transpose(0, 2, 1, 3).reshape(PAIRS, P, UNIT)
    parts = [token(w) for w in (q, k, v)] + [feature(w) for w in (ga, gb, c, x, b, w_out_b, w_out_a)] + [token(w_o)]
    parts.append(up[0:2])
    for j in range(1, PAIRS):
        parts += [up[2 * j:2 * j + 2], down[j - 1:j]]
    parts.append(down[PAIRS - 1:PAIRS])
    return np.concatenate(parts, axis=0)


def kernel(**inputs):
    import numpy as np
    import concourse.bacc as bacc
    from concourse import mybir as mb
    from concourse.bass_utils import run_bass_kernel_spmd

    a = {k: np.asarray(v) for k, v in inputs.items()}

    def columns(v, tiles):
        return v.reshape(tiles, P).T

    fw = a["ffn_conv_w"].reshape(3, 2, FT, P).transpose(3, 2, 1, 0).reshape(P, FT * 6)
    fb = a["ffn_conv_b"].reshape(2, FT, P).transpose(2, 1, 0).reshape(P, FT * 2)
    arrays = {
        "x": np.ascontiguousarray(a["x"][0]),
        "norm_ffn": a["norm_ffn"].reshape(1, D),
        "params": np.concatenate([a["conv_a_w"].reshape(3, KT, P).transpose(2, 1, 0).reshape(P, KT * 3),
                                  columns(a["q_norm"], 1), columns(a["k_norm"], 1), fw, fb,
                                  columns(a["norm_mix"], KT)], axis=1),
        "stream": weight_stream(a["w_in"], a["w_out_a"], a["w_out_b"], a["w_o"], a["w_up"], a["w_down"]),
    }
    nc = bacc.Bacc("TRN2", target_bir_lowering=False, num_devices=1)
    args = [nc.dram_tensor(n, v.shape, mb.dt.from_np(v.dtype), kind="ExternalInput").ap() for n, v in arrays.items()]
    args.append(nc.dram_tensor("out", (SEQ, D), F32, kind="ExternalOutput").ap())
    build(nc, *args)
    r = run_bass_kernel_spmd(nc, [arrays], core_ids=[0])
    return r.results[0]["out"].reshape(1, SEQ, D)
```
